# Optimizing a Trainium2 kernel written in Bass

```python
import math
import jax, jax.numpy as jnp
from jax import lax
import numpy as np

D_MODEL = 1024
BATCH = 1
SEQ = 256
DEPTH = 2

N_MEM = 256
N_MIXERS = 2
N_CONV_LAYERS = (DEPTH + 1) // 2
N_NSA_LAYERS = DEPTH // 2

CONV_WIDTH = 3

NSA_HEADS = 16
NSA_HEAD_DIM = D_MODEL // NSA_HEADS
NSA_KV_GROUPS = 4
NSA_HPG = NSA_HEADS // NSA_KV_GROUPS
CMP_BLOCK = 32
CMP_STRIDE = 16
CMP_HIDDEN = 2 * NSA_HEAD_DIM
SEL_BLOCK = 64
SEL_TOPK = 16
SEL_FORCE = 1.0e4
WINDOW = 512
Q_BLOCK = 128

XATTN_HEADS = 4
XATTN_HEAD_DIM = 128
XATTN_WIDTH = XATTN_HEADS * XATTN_HEAD_DIM
MIX_WIDTH = D_MODEL + XATTN_WIDTH

CONV_IN_WIDTH = 3 * D_MODEL + XATTN_WIDTH
NSA_IN_WIDTH = (NSA_HEADS * NSA_HEAD_DIM + 6 * NSA_KV_GROUPS * NSA_HEAD_DIM
                + 3 * NSA_HEADS + XATTN_WIDTH)

FFN_HIDDEN = ((8 * D_MODEL + 3 * 256 - 1) // (3 * 256)) * 256

REL_BUCKETS = 32
REL_MAX_DIST = 128
RMS_EPS = 1e-6
NEG = -1e30

kernel_name = "hybrid_shortconv_nsa_interleaved"

def rmsnorm(x, g):
    xf = x.astype(jnp.float32)
    y = xf * lax.rsqrt(jnp.mean(xf * xf, axis=-1, keepdims=True) + RMS_EPS)
    return (y * g.astype(jnp.float32)).astype(x.dtype)

def t5_bucket(dist):
    n = jnp.maximum(dist, 0)
    max_exact = REL_BUCKETS // 2
    nf = jnp.maximum(n, 1).astype(jnp.float32)
    large = max_exact + (jnp.log(nf / max_exact) / math.log(REL_MAX_DIST / max_exact)
                         * (REL_BUCKETS - max_exact)).astype(jnp.int32)
    large = jnp.minimum(large, REL_BUCKETS - 1)
    return jnp.where(n < max_exact, n, large)

def masked_softmax(logits, mask):
    p = jax.nn.softmax(jnp.where(mask, logits, NEG), axis=-1)
    return jnp.where(mask, p, 0.0)

def short_conv_mixer(u_b, u_c, u_x, conv_w):
    s = u_x.shape[1]
    v = u_c * u_x
    vp = jnp.pad(v, ((0, 0), (CONV_WIDTH - 1, 0), (0, 0)))
    conv = vp[:, 0:s] * conv_w[0]
    for k in range(1, CONV_WIDTH):
        conv = conv + vp[:, k:k + s] * conv_w[k]
    return u_b * conv

def memory_attention(xq, mem_n, w_mem_kv):
    b, s, _ = xq.shape
    m = mem_n.shape[1]
    kv = mem_n @ w_mem_kv
    k = kv[..., :XATTN_WIDTH].reshape(b, m, XATTN_HEADS, XATTN_HEAD_DIM)
    v = kv[..., XATTN_WIDTH:].reshape(b, m, XATTN_HEADS, XATTN_HEAD_DIM)
    q = xq.reshape(b, s, XATTN_HEADS, XATTN_HEAD_DIM)
    logits = jnp.einsum('bshd,bmhd->bhsm', q, k).astype(jnp.float32) * (XATTN_HEAD_DIM ** -0.5)
    p = jax.nn.softmax(logits, axis=-1).astype(v.dtype)
    o = jnp.einsum('bhsm,bmhd->bshd', p, v)
    return o.reshape(b, s, XATTN_WIDTH)

def nsa_mixer(proj, cmp_pos_k, cmp_w1_k, cmp_w2_k, cmp_pos_v, cmp_w1_v, cmp_w2_v, rel_bias):
    b, s, _ = proj.shape
    H, G, HPG, DK = NSA_HEADS, NSA_KV_GROUPS, NSA_HPG, NSA_HEAD_DIM
    qw = H * DK
    kvw = G * DK
    q = proj[..., :qw].reshape(b, s, G, HPG, DK).transpose(0, 2, 3, 1, 4)
    kv = proj[..., qw:qw + 6 * kvw].reshape(b, s, 6, G, DK).transpose(2, 0, 3, 1, 4)
    gates = jax.nn.sigmoid(proj[..., qw + 6 * kvw:].astype(jnp.float32)).reshape(b, s, 3, H)
    k_cmp_raw, v_cmp_raw, k_slc, v_slc, k_win, v_win = kv[0], kv[1], kv[2], kv[3], kv[4], kv[5]

    n_cmp = (s - CMP_BLOCK) // CMP_STRIDE + 1
    cmp_start = jnp.arange(n_cmp) * CMP_STRIDE
    cmp_idx = cmp_start[:, None] + jnp.arange(CMP_BLOCK)[None, :]

    def compress(raw, pos, w1, w2):
        blocks = raw[:, :, cmp_idx] + pos
        hmid = jax.nn.silu(blocks.reshape(b, G, n_cmp, CMP_BLOCK * DK) @ w1)
        return hmid @ w2

    k_cmp = compress(k_cmp_raw, cmp_pos_k, cmp_w1_k, cmp_w2_k)
    v_cmp = compress(v_cmp_raw, cmp_pos_v, cmp_w1_v, cmp_w2_v)
    cmp_last = cmp_start + CMP_BLOCK - 1

    n_sel = s // SEL_BLOCK
    top_k = min(SEL_TOPK, n_sel)
    sel_start = jnp.arange(n_sel) * SEL_BLOCK
    overlap = jnp.clip(jnp.minimum(cmp_start[:, None] + CMP_BLOCK, sel_start[None, :] + SEL_BLOCK)
                       - jnp.maximum(cmp_start[:, None], sel_start[None, :]), 0, None)
    overlap = overlap.astype(jnp.float32) / CMP_BLOCK

    bias_tab = rel_bias.astype(jnp.float32).T.reshape(G, HPG, REL_BUCKETS)
    g_ix = jnp.arange(G)[None, :, None, None, None]
    h_ix = jnp.arange(HPG)[None, None, :, None, None]
    k_win_p = jnp.pad(k_win, ((0, 0), (0, 0), (WINDOW, 0), (0, 0)))
    v_win_p = jnp.pad(v_win, ((0, 0), (0, 0), (WINDOW, 0), (0, 0)))
    band = WINDOW + Q_BLOCK
    scale = DK ** -0.5
    gather_rows = jax.vmap(jax.vmap(lambda a, i: a[i]))
    sel_offsets = jnp.arange(SEL_BLOCK)
    sel_ids = jnp.arange(n_sel)

    def block_fn(c):
        q0 = c * Q_BLOCK
        qb = lax.dynamic_slice_in_dim(q, q0, Q_BLOCK, axis=3)
        t = q0 + jnp.arange(Q_BLOCK)

        d_cmp = t[:, None] - cmp_last[None, :]
        lg = (jnp.einsum('bghqd,bgcd->bghqc', qb, k_cmp).astype(jnp.float32) * scale
              + bias_tab[:, :, t5_bucket(d_cmp)])
        p_cmp = masked_softmax(lg, d_cmp >= 0)
        o_cmp = jnp.einsum('bghqc,bgcd->bghqd', p_cmp.astype(v_cmp.dtype), v_cmp)

        imp = jnp.einsum('bghqc,cj->bgqj', p_cmp, overlap)
        cur = t // SEL_BLOCK
        forced = ((sel_ids[None, :] == 0) | (sel_ids[None, :] == cur[:, None])
                  | (sel_ids[None, :] == cur[:, None] - 1))
        valid = sel_start[None, :] <= t[:, None]
        imp = jnp.where(forced, SEL_FORCE, jnp.where(valid, imp, -SEL_FORCE))
        _, sel_idx = lax.top_k(imp, top_k)
        tok = (sel_idx[..., None] * SEL_BLOCK + sel_offsets).reshape(b, G, Q_BLOCK, top_k * SEL_BLOCK)
        k_s = gather_rows(k_slc, tok)
        v_s = gather_rows(v_slc, tok)
        d_s = t[None, None, :, None] - tok
        bias_s = bias_tab[g_ix, h_ix, t5_bucket(d_s)[:, :, None]]
        lg = jnp.einsum('bghqd,bgqtd->bghqt', qb, k_s).astype(jnp.float32) * scale + bias_s
        p_s = masked_softmax(lg, (d_s >= 0)[:, :, None])
        o_slc = jnp.einsum('bghqt,bgqtd->bghqd', p_s.astype(v_s.dtype), v_s)

        k_w = lax.dynamic_slice_in_dim(k_win_p, q0, band, axis=2)
        v_w = lax.dynamic_slice_in_dim(v_win_p, q0, band, axis=2)
        pos = q0 - WINDOW + jnp.arange(band)
        d_w = t[:, None] - pos[None, :]
        mask_w = (d_w >= 0) & (d_w < WINDOW) & (pos[None, :] >= 0)
        lg = (jnp.einsum('bghqd,bgkd->bghqk', qb, k_w).astype(jnp.float32) * scale
              + bias_tab[:, :, t5_bucket(d_w)])
        p_w = masked_softmax(lg, mask_w)
        o_win = jnp.einsum('bghqk,bgkd->bghqd', p_w.astype(v_w.dtype), v_w)
        return jnp.stack([o_cmp, o_slc, o_win], axis=0)

    outs = lax.map(block_fn, jnp.arange(s // Q_BLOCK))
    outs = outs.transpose(2, 0, 5, 1, 3, 4, 6).reshape(b, s, 3, H, DK)
    o = jnp.sum(gates[..., None].astype(outs.dtype) * outs, axis=2)
    return o.reshape(b, s, H * DK)

def setup_inputs(seed: int = 0) -> dict:
    key = jax.random.key(seed)
    ks = jax.random.split(key, 24)
    nrm = lambda k, shape, fan_in: jax.random.normal(k, shape, jnp.float32) * (fan_in ** -0.5)
    gain = lambda k, shape: 1.0 + 0.1 * jax.random.normal(k, shape, jnp.float32)
    return {
        "x": jax.random.normal(ks[0], (BATCH, SEQ, D_MODEL), jnp.float32),
        "mem": jax.random.normal(ks[1], (BATCH, N_MEM, D_MODEL), jnp.float32),
        "norm_mix_g": gain(ks[2], (DEPTH, D_MODEL)),
        "norm_mem_g": gain(ks[3], (DEPTH, D_MODEL)),
        "norm_ffn_g": gain(ks[4], (DEPTH, D_MODEL)),
        "norm_final_g": gain(ks[5], (D_MODEL,)),
        "w_in_conv": nrm(ks[6], (N_CONV_LAYERS, D_MODEL, CONV_IN_WIDTH), D_MODEL),
        "conv_w": nrm(ks[7], (N_CONV_LAYERS, CONV_WIDTH, D_MODEL), CONV_WIDTH),
        "w_in_nsa": nrm(ks[8], (N_NSA_LAYERS, D_MODEL, NSA_IN_WIDTH), D_MODEL),
        "cmp_pos_k": 0.1 * jax.random.normal(ks[9], (N_NSA_LAYERS, CMP_BLOCK, NSA_HEAD_DIM), jnp.float32),
        "cmp_w1_k": nrm(ks[10], (N_NSA_LAYERS, CMP_BLOCK * NSA_HEAD_DIM, CMP_HIDDEN), CMP_BLOCK * NSA_HEAD_DIM),
        "cmp_w2_k": nrm(ks[11], (N_NSA_LAYERS, CMP_HIDDEN, NSA_HEAD_DIM), CMP_HIDDEN),
        "cmp_pos_v": 0.1 * jax.random.normal(ks[12], (N_NSA_LAYERS, CMP_BLOCK, NSA_HEAD_DIM), jnp.float32),
        "cmp_w1_v": nrm(ks[13], (N_NSA_LAYERS, CMP_BLOCK * NSA_HEAD_DIM, CMP_HIDDEN), CMP_BLOCK * NSA_HEAD_DIM),
        "cmp_w2_v": nrm(ks[14], (N_NSA_LAYERS, CMP_HIDDEN, NSA_HEAD_DIM), CMP_HIDDEN),
        "rel_bias": 0.5 * jax.random.normal(ks[15], (REL_BUCKETS, NSA_HEADS), jnp.float32),
        "w_mem_kv": nrm(ks[16], (DEPTH, D_MODEL, 2 * XATTN_WIDTH), D_MODEL),
        "w_out": nrm(ks[17], (DEPTH, MIX_WIDTH, D_MODEL), MIX_WIDTH),
        "w_ffn_in": nrm(ks[18], (DEPTH, D_MODEL, 2 * FFN_HIDDEN), D_MODEL),
        "w_ffn_out": nrm(ks[19], (DEPTH, FFN_HIDDEN, D_MODEL), FFN_HIDDEN),
    }

def reference(x, mem, norm_mix_g, norm_mem_g, norm_ffn_g, norm_final_g, w_in_conv, conv_w,
              w_in_nsa, cmp_pos_k, cmp_w1_k, cmp_w2_k, cmp_pos_v, cmp_w1_v, cmp_w2_v, rel_bias,
              w_mem_kv, w_out, w_ffn_in, w_ffn_out):
    h = x
    for i in range(DEPTH):
        a = i // N_MIXERS
        hn = rmsnorm(h, norm_mix_g[i])
        mem_n = rmsnorm(mem, norm_mem_g[i])
        if i % N_MIXERS == 0:
            proj = hn @ w_in_conv[a]
            tok = short_conv_mixer(proj[..., :D_MODEL], proj[..., D_MODEL:2 * D_MODEL],
                                   proj[..., 2 * D_MODEL:3 * D_MODEL], conv_w[a])
            xq = proj[..., 3 * D_MODEL:]
        else:
            proj = hn @ w_in_nsa[a]
            tok = nsa_mixer(proj[..., :NSA_IN_WIDTH - XATTN_WIDTH], cmp_pos_k[a], cmp_w1_k[a],
                            cmp_w2_k[a], cmp_pos_v[a], cmp_w1_v[a], cmp_w2_v[a], rel_bias)
            xq = proj[..., NSA_IN_WIDTH - XATTN_WIDTH:]
        mo = memory_attention(xq, mem_n, w_mem_kv[i])
        h = h + jnp.concatenate([tok, mo], axis=-1) @ w_out[i]
        hn = rmsnorm(h, norm_ffn_g[i])
        gu = hn @ w_ffn_in[i]
        h = h + (jax.nn.silu(gu[..., :FFN_HIDDEN]) * gu[..., FFN_HIDDEN:]) @ w_ffn_out[i]
    return rmsnorm(h, norm_final_g)


_drawn_inputs = setup_inputs


def setup_inputs(seed=0):
    import zlib

    import numpy as np

    out = dict(_drawn_inputs(seed))
    spreads = {}
    factors = {'norm_mem_g': 5.544,
     'cmp_pos_k': 64.0,
     'cmp_pos_v': 3.762,
     'cmp_w1_k': 4.014,
     'cmp_w2_k': 3.787,
     'rel_bias': 2.959}
    for name, (base, spread) in spreads.items():
        noise = np.random.default_rng([zlib.crc32(name.encode()), seed]).standard_normal(out[name].shape)
        drawn = base * np.exp(spread * noise) if base else spread * noise
        out[name] = __import__('jax').numpy.asarray(drawn.astype(out[name].dtype))
    for name, factor in factors.items():
        out[name] = (out[name] * factor).astype(out[name].dtype)
    return out
```

```python
from contextlib import ExitStack

import numpy as np

import concourse.bass as bass
from concourse import mybir

ALU = mybir.AluOpType
ACT = mybir.ActivationFunctionType
AX_X = mybir.AxisListType.X
F32 = mybir.dt.float32
F32R = mybir.dt.float32r

P = 128
D, S, M = 1024, 256, 256
KT = D // P
TT = S // P
XH = 4
H, G, HPG, DK = 16, 4, 4, 64
MIXT = (D + XH * P) // P
FT = 2816 // P
CB, CS = 32, 16
NC = (S - CB) // CS + 1
BUCKETS = 32
CHUNK = 8 * P
RING = 6
RAW = RING // 2
AHEAD = 5
EPS = 1e-6
NEG = -1e30
FFN_LOOPS = (FT - 4) // 2
SMALL = 16 * 7
XSCALE = float(P) ** -0.5
SCALE = float(DK) ** -0.5
DIST0 = S

PARTS = [("mem_k0", 4), ("mem_v0", 4), ("xq0", 4), ("conv", 3 * KT), ("out0", MIXT), ("ffn0", 3 * FT),
         ("mem_k1", 4), ("mem_v1", 4), ("xq1", 4), ("cmp_kv", 4), ("w1_k", 2), ("w1_v", 2), ("nat_v", 4), ("gates", 1),
         ("k_slc", 2), ("k_win", 2), ("q", 8), ("out1", MIXT), ("ffn1", 3 * FT)]
START, TOTAL = {}, 0
for _name, _count in PARTS:
    START[_name] = TOTAL
    TOTAL += _count


def build(nc, stream, xT, memT, gains, conv_w, cmp_pos, cmp_w2, rel_bias, dist_fwd, ident, outT):
    table_dram = nc.dram_tensor("bias_by_distance", (H, 2 * S), F32, kind="Internal").ap()
    with ExitStack() as ctx:
        def sb(name, shape, dt=F32):
            return ctx.enter_context(nc.sbuf_tensor(name, shape, dt))

        def sem(name):
            return ctx.enter_context(nc.semaphore(name))

        raw = sb("raw", [P, RAW, CHUNK])
        w_hi = sb("w_hi", [P, RING, CHUNK], F32R)
        w_lo = sb("w_lo", [P, RING, CHUNK], F32R)
        h = sb("h", [P, KT, S])
        mem = sb("mem", [P, KT, M])
        n_hi = sb("n_hi", [P, KT, S], F32R)
        n_lo = sb("n_lo", [P, KT, S], F32R)
        mix_hi = sb("mix_hi", [P, MIXT, S], F32R)
        mix_lo = sb("mix_lo", [P, MIXT, S], F32R)
        m_hi, m_lo = mix_hi[:, 0:KT], mix_lo[:, 0:KT]
        sq = sb("sq", [P, 2, S])
        rms = sb("rms", [P, S])
        rstd = sb("rstd", [P, S])
        mem_rstd = sb("mem_rstd", [P, M])
        normed = sb("normed", [P, 2, S])
        gain = sb("gain", [P, 7, KT])
        taps = sb("taps", [P, 3, KT])
        ones = sb("ones", [P, P])
        idt = sb("idt", [P, P])
        eps = sb("eps", [P, 1])
        tab = sb("tab", [BUCKETS + 1, H])
        bias = sb("bias", [P, H, S])
        bias_c = sb("bias_c", [P, TT, H, NC])
        pos = sb("pos", [P, 2, CS])
        w2 = sb("w2", [P, 2, P])
        xq = sb("xq", [P, XH, S])
        mk = sb("mk", [P, XH, M])
        mv = sb("mv", [P, 2, XH * P])
        c_sb = sb("c_sb", [P, 2, S])
        vpad = sb("vpad", [P, 2, S + 2])
        conv = sb("conv", [P, 2, S])
        silu = sb("silu", [P, 2, S])
        hid = sb("hid", [P, 2, S])
        hid_hi = sb("hid_hi", [P, 2, S], F32R)
        hid_lo = sb("hid_lo", [P, 2, S], F32R)
        q_sb = mem
        ks = sb("ks", [P, 2, 2, S])
        v_nat = sb("v_nat", [P, TT, 2, G, DK])
        gate = sb("gate", [P, TT, 3, H])
        r_hi = sb("r_hi", [P, CS, G, NC], F32R)
        r_lo = sb("r_lo", [P, CS, G, NC], F32R)
        hmid = sb("hmid", [P, 2, G * NC])
        kc = sb("kc", [P, G, NC])
        vc = sb("vc", [P, G, HPG * DK])
        lc = sb("lc", [P, H, NC])
        pc = sb("pc", [P, TT, H, 32])
        pcT = xq[:].rearrange("p h (t q) -> p (h t) q", q=P)
        logit = sb("logit", [P, 2, 2, S])
        prob = sb("prob", [P, 2, 2, S])
        probT = sb("probT", [P, 2, 4, P])
        fwd = logit[0:BUCKETS + 1, 1].rearrange("p b s -> p (b s)")
        tab_row = prob[0:H, 0].rearrange("p b s -> p (b s)")
        r_raw = logit[:].rearrange("p a b s -> p (a b s)")[:, 0:CS * G * NC]\
            .rearrange("p (l g c) -> p l g c", l=CS, g=G)
        o_nat = mk[:, 0:2]
        col = sb("col", [P, 2, 16])
        colc = sb("colc", [P, 4, H])

        bank = [ctx.enter_context(nc.psum_tensor(f"bank{i}", [P, 512], F32)) for i in range(8)]

        raw_loaded = [sem(f"raw_loaded{i}") for i in range(RAW)]
        hi_ready = sem("hi_ready")
        lo_ready = sem("lo_ready")
        chunk_done = sem("chunk_done")
        x_loaded = sem("x_loaded")
        mem_loaded = sem("mem_loaded")
        small_loaded = sem("small_loaded")
        consts_set = sem("consts_set")
        table_ready = sem("table_ready")
        table_copied = sem("table_copied")
        table_stored = sem("table_stored")
        bias_loaded = sem("bias_loaded")
        dve_step = sem("dve_step")
        act_step = sem("act_step")
        out_ready = sem("out_ready")
        out_stored = sem("out_stored")

        NORMS = ["mem0", "x0", "f0", "mem1", "x1", "f1", "end"]
        sq_ready = sem("sq_ready")
        sq_used = sem("sq_used")
        rms_ready = sem("rms_ready")
        normed_ready = sem("normed_ready")
        n_hi_ready = sem("n_hi_ready")
        n_lo_ready = sem("n_lo_ready")
        residual_added = sem("residual_added")

        tile_copied = sem("tile_copied")
        x_score = sem("x_score")
        x_max = sem("x_max")
        x_exp = sem("x_exp")
        x_prob = sem("x_prob")
        x_turned = sem("x_turned")
        x_copied = sem("x_copied")
        x_o = sem("x_o")
        x_o_hi = sem("x_o_hi")
        x_o_lo = sem("x_o_lo")
        c_copied = sem("c_copied")
        tok_ready = sem("tok_ready")
        tok_hi = sem("tok_hi")
        tok_lo = sem("tok_lo")
        silu_ready = sem("silu_ready")
        hid_ready = sem("hid_ready")
        hid_hi_ready = sem("hid_hi_ready")
        hid_lo_ready = sem("hid_lo_ready")
        blocks_ready = sem("blocks_ready")
        blocks_hi = sem("blocks_hi")
        blocks_lo = sem("blocks_lo")
        hmid_ready = sem("hmid_ready")
        kvc_ready = sem("kvc_ready")
        kvc_copied = sem("kvc_copied")
        gate_exp = sem("gate_exp")
        sc_ready = sem("sc_ready")
        lc_ready = sem("lc_ready")
        lc_exp = sem("lc_exp")
        pc_ready = sem("pc_ready")
        pcT_ready = sem("pcT_ready")
        pcT_copied = sem("pcT_copied")
        score = sem("score")
        logit_ready = sem("logit_ready")
        exp_ready = sem("exp_ready")
        prob_ready = sem("prob_ready")
        turned = sem("turned")
        probT_ready = sem("probT_ready")
        pv_done = sem("pv_done")
        o_copied = sem("o_copied")
        oT_ready = sem("oT_ready")
        oT_hi = sem("oT_hi")
        oT_lo = sem("oT_lo")

        def f32(ap):
            return ap.bitcast(F32)

        SUMMED = ["mem0", "x0", "f0", "x1", "f1", "end"]

        def norm_source(name):
            return mem if name.startswith("mem") else h

        X_UNITS = [(a, t) for a in range(XH) for t in range(TT)]
        N_UNITS = [(g, t, a) for g in range(G) for t in range(TT) for a in range(HPG)]

        def cmp_bank(t, odd):
            return bank[2 * (1 - odd) + t]

        block = ctx.enter_context(nc.Block())

        @block.sync
        def _(sp):
            sp.dma_start(mem[:], memT).then_inc(mem_loaded, 16)
            sp.dma_start(gain[:], gains).then_inc(small_loaded, 16)
            sp.dma_start(h[:], xT).then_inc(x_loaded, 16)

            def load(c, slot):
                sp.dma_start(raw[:, slot], stream[c]).then_inc(raw_loaded[slot], 16)

            for tile, src in ((taps, conv_w), (idt, ident), (pos, cmp_pos), (w2, cmp_w2), (fwd, dist_fwd)):
                sp.dma_start(tile if tile is fwd else tile[:], src).then_inc(small_loaded, 16)
            sp.dma_start(tab[0:BUCKETS, :], rel_bias).then_inc(small_loaded, 16)
            for c in range(RAW):
                load(c, c)
            full = TOTAL // RAW
            with sp.Fori(1, full) as i:
                for slot in range(RAW):
                    sp.wait_ge(lo_ready, i * RAW + (slot + 1 - RAW))
                    load(i * RAW + slot, slot)
            for c in range(full * RAW, TOTAL):
                sp.wait_ge(lo_ready, c - RAW + 1)
                load(c, c % RAW)
            for m in range(KT):
                sp.wait_ge(out_ready, m + 1)
                sp.dma_start(outT[:, m], mem[:, m]).then_inc(out_stored, 16)
            sp.wait_ge(out_stored, 16 * KT)

        @block.gpsimd
        def _(pool):
            for n, (tile, value) in enumerate(((ones, 1.0), (eps, EPS), (vpad, 0.0),
                                               (tab[BUCKETS:BUCKETS + 1, :], NEG), (pc, 0.0), (vc, 0.0))):
                if n:
                    pool.wait_ge(consts_set, n)
                nc.gpsimd.memset(tile if tile.shape[0] == 1 else tile[:], value).then_inc(consts_set, 1)
            pool.wait_ge(table_copied, 1)
            pool.dma_start(table_dram, tab_row).then_inc(table_stored, 16)
            pool.wait_ge(table_stored, 16)
            rows = bass.AP(tensor=table_dram.tensor, offset=DIST0 - (P - 1), ap=[[1, P], [2 * S, H], [1, S]])
            pool.dma_start(bias[:], rows).then_inc(bias_loaded, 16)
            pool.wait_ge(bias_loaded, 16)

        @block.scalar
        def _(act):
            split = [0]

            def split_hi(c, slot, landed, may_wait=True):
                act.wait_ge(raw_loaded[slot % RAW], landed)
                if may_wait:
                    act.wait_ge(chunk_done, c - RING + 1)
                nc.scalar.copy(w_hi[:, slot], raw[:, slot % RAW]).then_inc(hi_ready, 1)

            def split_to(end):
                while split[0] < min(end, TOTAL):
                    c = split[0]
                    split_hi(c, c % RING, 16 * (c // RAW + 1), c >= RING)
                    split[0] += 1

            def split_loop(i, k, count):
                for _ in range(count):
                    c = split[0] + k[0]
                    split_hi(i * RING + c, c % RING, i * (16 * RING // RAW) + 16 * (c // RAW + 1))
                    k[0] += 1

            def copy_tiles(part, outs, scale=1.0):
                for n, out in enumerate(outs):
                    c = START[part] + n
                    split_to(c + 1 + AHEAD)
                    act.wait_ge(chunk_done, c + 1)
                    nc.scalar.mul(out, bank[n % 2][:, 0:S], scale).then_inc(tile_copied, 1)

            def copy_rows(part, outs):
                split_to(START[part] + 4 + AHEAD)
                act.wait_ge(chunk_done, START[part] + 4)
                for t, out in enumerate(outs):
                    nc.scalar.copy(out, bank[t][:]).then_inc(tile_copied, 1)

            squares = [0]
            hi_norms = [0]

            def norm(name):
                src = norm_source(name)
                if name in SUMMED:
                    for m in range(KT):
                        n = squares[0]
                        if name == "mem0":
                            act.wait_ge(mem_loaded, 16)
                        elif name == "x0":
                            act.wait_ge(x_loaded, 16)
                        else:
                            act.wait_ge(residual_added, KT // 2 * (SUMMED.index(name) - 2) + m // 2 + 1)
                        if n >= 2:
                            act.wait_ge(sq_used, n - 1)
                        nc.scalar.activation(sq[:, n % 2], src[:, m], ACT.Square).then_inc(sq_ready, 1)
                        squares[0] += 1
                    act.wait_ge(sq_used, squares[0])
                    act.wait_ge(consts_set, 6)
                    nc.scalar.activation(rms[:], bank[7][:, 0:S], ACT.Sqrt, bias=eps[:, 0:1],
                                         scale=1.0 / D).then_inc(rms_ready, 1)
                if name == "end":
                    return
                hi = m_hi if name.startswith("mem") else n_hi
                for m in range(KT):
                    act.wait_ge(normed_ready, hi_norms[0] + 1)
                    nc.scalar.copy(hi[:, m], normed[:, hi_norms[0] % 2]).then_inc(n_hi_ready, 1)
                    hi_norms[0] += 1

            def memory_attention(layer):
                base = layer * len(X_UNITS)

                def turn(n):
                    head, t = X_UNITS[n]
                    act.wait_ge(x_turned, base + n + 1)
                    nc.scalar.copy(probT[:, head % 2].rearrange("p (m t) q -> p m t q", t=2)[:, :, t],
                                   bank[4 + n % 2][:, 0:256].rearrange("p (m q) -> p m q", m=2))\
                        .then_inc(x_copied, 1)

                def output(n):
                    head, t = X_UNITS[n]
                    if t == 1:
                        act.wait_ge(x_o, layer * XH + head + 1)
                        nc.scalar.copy(mix_hi[:, KT + head], bank[6][:, 0:S]).then_inc(x_o_hi, 1)

                for n, (head, t) in enumerate(X_UNITS):
                    act.wait_ge(x_max, base + n + 1)
                    nc.scalar.activation(prob[:, n % 2, 0], bank[2 + n % 2][:, 0:M], ACT.Exp,
                                         bias=col[:, n % 2, 1:2], scale=XSCALE,
                                         accum_out=col[:, n % 2, 2:3]).then_inc(x_exp, 1)
                    if n >= 1:
                        turn(n - 1)
                    if n >= 2:
                        output(n - 2)
                turn(len(X_UNITS) - 1)
                output(len(X_UNITS) - 1)

            def ffn(layer):
                base = START[f"ffn{layer}"]

                def tile(f, parity, done):
                    count = f + (layer * FT + 1)
                    act.wait_ge(chunk_done, done)
                    nc.scalar.activation(silu[:, parity], bank[4 + parity][:, 0:S], ACT.Silu).then_inc(silu_ready, 1)
                    act.wait_ge(hid_ready, count)
                    nc.scalar.copy(hid_hi[:, parity], hid[:, parity]).then_inc(hid_hi_ready, 1)

                split_to(base + 2 + AHEAD)
                tile(0, 0, base + 2)
                split_to(base + 4 + AHEAD)
                tile(1, 1, base + 4)
                if layer == 0:
                    norm("mem1")
                split_to(base + 5 + AHEAD)
                with act.Fori(0, FFN_LOOPS) as i:
                    k = [0]
                    for j in (0, 1):
                        split_loop(i, k, 2)
                        tile(i * 2 + (2 + j), j, i * RING + (base + 5 + 3 * j + 2))
                        split_loop(i, k, 1)
                split[0] += FFN_LOOPS * RING
                for f in (FT - 2, FT - 1):
                    split_to(base + 3 * f + 1 + AHEAD)
                    tile(f, f % 2, base + 3 * f + 1)

            norm("mem0")
            split_to(AHEAD)
            norm("x0")
            copy_tiles("mem_k0", [mk[:, n] for n in range(XH)])
            copy_rows("mem_v0", [mv[:, t] for t in range(2)])
            copy_tiles("xq0", [xq[:, n] for n in range(XH)])

            split_to(START["conv"] + AHEAD)
            with act.Fori(0, KT // 2) as i:
                k = [0]
                for j in (0, 1):
                    split_loop(i, k, 2)
                    act.wait_ge(chunk_done, i * RING + (START["conv"] + 3 * j + 2))
                    nc.scalar.copy(c_sb[:, j], bank[j][:, 0:S]).then_inc(c_copied, 1)
                    split_loop(i, k, 1)
                    act.wait_ge(tok_ready, i * 2 + (j + 1))
                    nc.scalar.copy(mix_hi[:, bass.ds(i * 2 + j, 1)], conv[:, j:j + 1]).then_inc(tok_hi, 1)
            split[0] += 3 * KT
            act.wait_ge(table_stored, 16)
            memory_attention(0)
            split_to(START["ffn0"] + AHEAD)
            norm("f0")
            ffn(0)

            norm("x1")
            copy_tiles("mem_k1", [mk[:, n] for n in range(XH)])
            copy_rows("mem_v1", [mv[:, t] for t in range(2)])
            copy_tiles("xq1", [xq[:, n] for n in range(XH)])
            for kv in range(2):
                split_to(START["cmp_kv"] + 2 * kv + 2 + AHEAD)
                act.wait_ge(blocks_ready, kv + 1)
                nc.scalar.copy(r_hi[:], r_raw[:]).then_inc(blocks_hi, 1)
                split_to(START["w1_k"] + 2 * kv + 2 + AHEAD)
                act.wait_ge(chunk_done, START["w1_k"] + 2 * kv + 2)
                nc.scalar.activation(hmid[:, kv], bank[2][:, 0:G * NC], ACT.Silu).then_inc(hmid_ready, 1)
            copy_rows("nat_v", [v_nat[:, t].rearrange("p b g d -> p (b g d)") for t in range(TT)])
            split_to(START["gates"] + 1 + AHEAD)
            act.wait_ge(chunk_done, START["gates"] + 1)
            nc.scalar.activation(gate[:].rearrange("p t b h -> p (t b h)"), bank[3][:, 0:TT * 3 * H],
                                 ACT.Exp, scale=-1.0).then_inc(gate_exp, 1)
            copy_tiles("k_slc", [ks[:, 0, a] for a in range(2)])
            copy_tiles("k_win", [ks[:, 1, a] for a in range(2)])
            copy_tiles("q", [q_sb[:, n] for n in range(8)], scale=SCALE)
            memory_attention(1)
            for t in range(TT):
                act.wait_ge(lc_ready, t + 1)
                nc.scalar.activation(lc[:], lc[:], ACT.Exp).then_inc(lc_exp, 1)
            def turn(n):
                g, t, a = N_UNITS[n]
                act.wait_ge(turned, n + 1)
                if n >= 2:
                    act.wait_ge(pv_done, n - 1)
                blocks = 2 * (t + 1)
                nc.scalar.copy(probT[:, n % 2, 0:blocks],
                               bank[4 + n % 2][:, 0:blocks * P].rearrange("p (b q) -> p b q", q=P))\
                    .then_inc(probT_ready, 1)

            def output(n):
                g, t, a = N_UNITS[n]
                if a == HPG - 1:
                    act.wait_ge(oT_ready, g * TT + t + 1)
                    for half in range(2):
                        nc.scalar.copy(mix_hi[:, 2 * g + half, t * P:(t + 1) * P],
                                       bank[7][:, half * P:(half + 1) * P]).then_inc(oT_hi, 1)

            for n in range(len(N_UNITS) + 4):
                if n < len(N_UNITS):
                    g, t, a = N_UNITS[n]
                    keys = (t + 1) * P
                    act.wait_ge(logit_ready, n + 1)
                    for b in range(2):
                        nc.scalar.activation(prob[:, n % 2, b, 0:keys], logit[:, n % 2, b, 0:keys], ACT.Exp,
                                             bias=col[:, n % 2, 2 + b:3 + b],
                                             accum_out=col[:, n % 2, 4 + b:5 + b]).then_inc(exp_ready, 1)
                if 1 <= n <= len(N_UNITS):
                    turn(n - 1)
                if n >= 4:
                    output(n - 4)
            split_to(START["ffn1"] + AHEAD)
            norm("f1")
            ffn(1)
            norm("end")

        @block.vector
        def _(dve):
            split = [0]
            steps = [0]

            def link(ins):
                steps[0] += 1
                ins.then_inc(dve_step, 1)
                dve.wait_ge(dve_step, steps[0])

            def split_lo(c, slot):
                dve.wait_ge(hi_ready, c + 1)
                nc.vector.tensor_tensor(w_lo[:, slot], raw[:, slot % RAW], f32(w_hi[:, slot]), ALU.subtract)\
                    .then_inc(lo_ready, 1)

            def split_to(end):
                while split[0] < min(end, TOTAL):
                    split_lo(split[0], split[0] % RING)
                    split[0] += 1

            def split_loop(i, k, count):
                for _ in range(count):
                    c = split[0] + k[0]
                    split_lo(i * RING + c, c % RING)
                    k[0] += 1

            norms = [0]

            def add_residual(part):
                dve.wait_ge(chunk_done, START[part] + dict(PARTS)[part])
                for b in range(4):
                    hh = h[:, 2 * b:2 * b + 2]
                    nc.vector.tensor_tensor(hh, bank[b][:].rearrange("p (m s) -> p m s", m=2), hh, ALU.add)\
                        .then_inc(residual_added, 1)

            def norm(name):
                src = norm_source(name)
                if name in SUMMED:
                    dve.wait_ge(rms_ready, SUMMED.index(name) + 1)
                    dst = mem_rstd if name == "mem0" else rstd
                    link(nc.vector.reciprocal(dst[:], rms[:]))
                r = mem_rstd if name.startswith("mem") else rstd
                gcol = NORMS.index(name)
                lo, hi = (m_lo, m_hi) if name.startswith("mem") else (n_lo, n_hi)

                def low(m, n):
                    dve.wait_ge(n_hi_ready, n + 1)
                    nc.vector.tensor_tensor(lo[:, m], normed[:, n % 2], f32(hi[:, m]), ALU.subtract)\
                        .then_inc(n_lo_ready, 1)

                if name == "mem0":
                    dve.wait_ge(small_loaded, SMALL)
                    dve.wait_ge(consts_set, 6)
                for m in range(KT):
                    n = norms[0]
                    out, done = (mem[:, m], out_ready) if name == "end" else (normed[:, n % 2], normed_ready)
                    if name != "end" and n >= 2:
                        dve.wait_ge(n_lo_ready, n - 1)
                    nc.vector.scalar_tensor_tensor(out=out, in0=src[:, m],
                                                   scalar=gain[:, gcol, m:m + 1], in1=r[:],
                                                   op0=ALU.mult, op1=ALU.mult).then_inc(done, 1)
                    if name != "end" and m >= 1:
                        low(m - 1, n - 1)
                    norms[0] += 1
                if name != "end":
                    low(KT - 1, norms[0] - 1)

            def memory_attention(layer):
                base = layer * len(X_UNITS)

                def finish(n):
                    head, t = X_UNITS[n]
                    if t == 1:
                        k = layer * XH + head
                        dve.wait_ge(x_o_hi, k + 1)
                        nc.vector.tensor_tensor(mix_lo[:, KT + head], bank[6][:, 0:S],
                                                f32(mix_hi[:, KT + head]), ALU.subtract).then_inc(x_o_lo, 1)

                for n in range(len(X_UNITS)):
                    k = n % 2
                    dve.wait_ge(x_score, base + n + 1)
                    link(nc.vector.reduce_max(col[:, k, 0:1], bank[2 + k][:, 0:M], AX_X))
                    nc.vector.tensor_scalar(col[:, k, 1:2], col[:, k, 0:1], -XSCALE, None, ALU.mult)\
                        .then_inc(x_max, 1)
                    dve.wait_ge(x_exp, base + n + 1)
                    link(nc.vector.reciprocal(col[:, k, 3:4], col[:, k, 2:3]))
                    nc.vector.tensor_scalar(prob[:, k, 0], prob[:, k, 0], col[:, k, 3:4], None, ALU.mult)\
                        .then_inc(x_prob, 1)
                    if n >= 3:
                        finish(n - 3)
                for n in range(len(X_UNITS) - 3, len(X_UNITS)):
                    finish(n)

            def ffn(layer):
                base = START[f"ffn{layer}"]

                def tile(f, parity):
                    count = f + (layer * FT + 1)
                    dve.wait_ge(silu_ready, count)
                    if not (layer == 0 and isinstance(f, int) and f < 2):
                        dve.wait_ge(hid_lo_ready, count - 2)
                    nc.vector.tensor_tensor(hid[:, parity], bank[4 + parity][:, S:2 * S], silu[:, parity], ALU.mult)\
                        .then_inc(hid_ready, 1)
                    dve.wait_ge(hid_hi_ready, count)
                    nc.vector.tensor_tensor(hid_lo[:, parity], hid[:, parity], f32(hid_hi[:, parity]), ALU.subtract)\
                        .then_inc(hid_lo_ready, 1)

                split_to(base + 2 + AHEAD)
                tile(0, 0)
                split_to(base + 4 + AHEAD)
                tile(1, 1)
                if layer == 0:
                    norm("mem1")
                split_to(base + 5 + AHEAD)
                with dve.Fori(0, FFN_LOOPS) as i:
                    k = [0]
                    for j in (0, 1):
                        split_loop(i, k, 2)
                        tile(i * 2 + (2 + j), j)
                        split_loop(i, k, 1)
                split[0] += FFN_LOOPS * RING
                for f in (FT - 2, FT - 1):
                    split_to(base + 3 * f + 1 + AHEAD)
                    tile(f, f % 2)

            norm("mem0")
            split_to(AHEAD)
            norm("x0")
            split_to(START["mem_k0"] + 4 + AHEAD)
            dve.wait_ge(table_ready, 1)
            nc.vector.tensor_copy(tab_row, bank[2][0:H, :]).then_inc(table_copied, 1)
            nc.vector.tensor_copy(bias_c[:].rearrange("p t h c -> p t c h"),
                                  bank[3][:, 0:TT * NC * H].rearrange("p (t c h) -> p t c h", t=TT, c=NC))\
                .then_inc(table_copied, 1)
            split_to(START["conv"] + AHEAD)
            per = 2 * 4
            conv_steps = steps[0]
            with dve.Fori(0, KT // 2) as i:
                k = [0]
                done = [0]

                def chain(ins):
                    done[0] += 1
                    ins.then_inc(dve_step, 1)
                    dve.wait_ge(dve_step, i * per + (conv_steps + done[0]))

                for j in (0, 1):
                    ft = i * 2 + j
                    split_loop(i, k, 2)
                    dve.wait_ge(c_copied, ft + 1)
                    chain(nc.vector.tensor_tensor(vpad[:, j, 2:S + 2], bank[j][:, S:2 * S], c_sb[:, j], ALU.mult))
                    chain(nc.vector.tensor_scalar(conv[:, j], vpad[:, j, 0:S], taps[:, 0, bass.ds(ft, 1)], None, ALU.mult))
                    for tap in (1, 2):
                        chain(nc.vector.scalar_tensor_tensor(out=conv[:, j], in0=vpad[:, j, tap:tap + S],
                                                             scalar=taps[:, tap, bass.ds(ft, 1)], in1=conv[:, j],
                                                             op0=ALU.mult, op1=ALU.add))
                    split_loop(i, k, 1)
                    dve.wait_ge(chunk_done, i * RING + (START["conv"] + 3 * j + 3))
                    nc.vector.tensor_tensor(conv[:, j], bank[4 + j][:, 0:S], conv[:, j], ALU.mult).then_inc(tok_ready, 1)
                    dve.wait_ge(tok_hi, ft + 1)
                    nc.vector.tensor_tensor(mix_lo[:, bass.ds(ft, 1)], conv[:, j:j + 1], f32(mix_hi[:, bass.ds(ft, 1)]),
                                            ALU.subtract).then_inc(tok_lo, 1)
                    dve.wait_ge(tok_lo, ft + 1)
                assert done[0] == per
            steps[0] += per * (KT // 2)
            split[0] += 3 * KT
            memory_attention(0)
            split_to(START["ffn0"] + AHEAD)
            add_residual("out0")
            norm("f0")
            ffn(0)
            add_residual("ffn0")

            norm("x1")
            split_to(START["xq1"] + 4 + AHEAD)
            for kv in range(2):
                split_to(START["cmp_kv"] + 2 * kv + 2 + AHEAD)
                if kv:
                    dve.wait_ge(blocks_lo, kv)
                for pair in range(2):
                    dve.wait_ge(chunk_done, START["cmp_kv"] + 2 * kv + pair + 1)
                    for gg in range(2):
                        for half in range(2):
                            src = bank[pair][64 * gg:64 * gg + 64, CS * half:CS * (half + NC)]
                            at = slice(64 * half, 64 * half + 64)
                            ins = nc.vector.tensor_tensor(
                                r_raw[at, :, 2 * pair + gg], src.rearrange("p (c l) -> p l c", l=CS),
                                pos[at, kv, :, None].to_broadcast([64, CS, NC]), ALU.add)
                ins.then_inc(blocks_ready, 1)
                dve.wait_ge(blocks_hi, kv + 1)
                if kv == 1:
                    dve.wait_ge(chunk_done, START["w1_k"] + 2)
                nc.vector.tensor_tensor(r_lo[:], r_raw[:], f32(r_hi[:]), ALU.subtract).then_inc(blocks_lo, 1)
                split_to(START["w1_k"] + 2 * kv + 2 + AHEAD)
                dve.wait_ge(kvc_ready, kv + 1)
                if kv == 0:
                    nc.vector.tensor_copy(kc[:], bank[3][:, 0:G * NC].rearrange("p (g c) -> p g c", g=G))\
                        .then_inc(kvc_copied, 1)
                else:
                    dve.wait_ge(consts_set, 6)
                    for a in range(HPG):
                        nc.vector.tensor_copy(vc[32 * a:32 * a + NC, :, a * DK:(a + 1) * DK],
                                              bank[3][0:NC, 0:G * DK].rearrange("p (g d) -> p g d", g=G))\
                            .then_inc(kvc_copied, 1)
            split_to(START["gates"] + 1 + AHEAD)
            dve.wait_ge(gate_exp, 1)
            link(nc.vector.tensor_scalar(gate[:], gate[:], 1.0, None, ALU.add))
            link(nc.vector.reciprocal(gate[:], gate[:]))
            split_to(START["q"] + 8 + AHEAD)
            memory_attention(1)
            for t in range(TT):
                dve.wait_ge(sc_ready, t + 1)
                if t:
                    dve.wait_ge(pc_ready, t)
                for odd in range(2):
                    def part(x):
                        return x.rearrange("p (g o a) c -> p g o (a c)", g=G // 2, o=2)[:, :, odd]
                    ins = nc.vector.tensor_tensor(part(lc[:]), cmp_bank(t, odd)[:, 0:H * NC // 2].rearrange(
                        "p (g x) -> p g x", g=G // 2), part(bias_c[:, t]), ALU.add)
                link(ins)
                link(nc.vector.reduce_max(colc[:, 0], lc[:], AX_X))
                link(nc.vector.tensor_scalar(colc[:, 1], colc[:, 0], NEG / 10, None, ALU.max))
                nc.vector.tensor_tensor(lc[:], lc[:], colc[:, 1, :, None].to_broadcast([P, H, NC]), ALU.subtract)\
                    .then_inc(lc_ready, 1)
                dve.wait_ge(lc_exp, t + 1)
                link(nc.vector.reduce_sum(colc[:, 2], lc[:], AX_X))
                link(nc.vector.tensor_scalar(colc[:, 2], colc[:, 2], 1e-30, None, ALU.max))
                link(nc.vector.reciprocal(colc[:, 3], colc[:, 2]))
                link(nc.vector.tensor_tensor(colc[:, 3], colc[:, 3], gate[:, t, 0], ALU.mult))
                nc.vector.tensor_tensor(pc[:, t, :, 0:NC], lc[:], colc[:, 3, :, None].to_broadcast([P, H, NC]), ALU.mult)\
                    .then_inc(pc_ready, 1)
            for half in range(2):
                dve.wait_ge(pcT_ready, half + 1)
                nc.vector.tensor_copy(pcT[:, 4 * half:4 * half + 4], bank[4 + half][:].rearrange("p (u q) -> p u q", q=P))\
                    .then_inc(pcT_copied, 1)

            def copy_output(n):
                g, t, a = N_UNITS[n]
                if a == HPG - 1:
                    u = g * TT + t
                    dve.wait_ge(pv_done, n + 1)
                    if u >= 2:
                        dve.wait_ge(oT_ready, u - 1)
                    nc.vector.tensor_copy(o_nat[:, u % 2], bank[6][:, 0:HPG * DK]).then_inc(o_copied, 1)

            def output(n):
                g, t, a = N_UNITS[n]
                if a == HPG - 1:
                    u, at = g * TT + t, slice(t * P, (t + 1) * P)
                    dve.wait_ge(oT_hi, 2 * u + 2)
                    for half in range(2):
                        nc.vector.tensor_tensor(mix_lo[:, 2 * g + half, at], bank[7][:, half * P:(half + 1) * P],
                                                f32(mix_hi[:, 2 * g + half, at]), ALU.subtract).then_inc(oT_lo, 1)

            dve.wait_ge(bias_loaded, 16)
            for n in range(len(N_UNITS) + 5):
                if n < len(N_UNITS):
                    g, t, a = N_UNITS[n]
                    k, keys, head = n % 2, (t + 1) * P, g * HPG + a
                    dve.wait_ge(score, n + 1)
                    link(nc.vector.tensor_tensor(logit[:, k, :, 0:keys],
                                                 bank[2 + k][:].rearrange("p (b s) -> p b s", b=2)[:, :, 0:keys],
                                                 bias[:, head, None, keys - 1::-1].to_broadcast([P, 2, keys]), ALU.add))
                    link(nc.vector.reduce_max(col[:, k, 0:2], logit[:, k, :, 0:keys], AX_X))
                    nc.vector.tensor_scalar(col[:, k, 2:4], col[:, k, 0:2], -1.0, None, ALU.mult).then_inc(logit_ready, 1)
                    dve.wait_ge(exp_ready, 2 * n + 2)
                    link(nc.vector.reciprocal(col[:, k, 6:8], col[:, k, 4:6]))
                    link(nc.vector.tensor_tensor(col[:, k, 8:10], col[:, k, 6:8], gate[:, t, 1:3, head], ALU.mult))
                    for b in range(2):
                        ins = nc.vector.tensor_scalar(prob[:, k, b, 0:keys], prob[:, k, b, 0:keys],
                                                      col[:, k, 8 + b:9 + b], None, ALU.mult)
                    ins.then_inc(prob_ready, 1)
                if 3 <= n < len(N_UNITS) + 3:
                    copy_output(n - 3)
                if n >= 5:
                    output(n - 5)
            split_to(START["ffn1"] + AHEAD)
            add_residual("out1")
            norm("f1")
            ffn(1)
            add_residual("ffn1")
            norm("end")

        @block.tensor
        def _(pe):
            def three_passes(out, slot, cols, x_hi, x_lo, start, stop, **kw):
                nc.tensor.matmul(out, w_hi[:, slot, cols], x_hi, start=start, stop=False, **kw)
                nc.tensor.matmul(out, w_hi[:, slot, cols], x_lo, start=False, stop=False, **kw)
                return nc.tensor.matmul(out, w_lo[:, slot, cols], x_hi, start=False, stop=stop, **kw)

            def project(c, slot, out, x_hi, x_lo):
                pe.wait_ge(lo_ready, c + 1)
                for kt in range(KT):
                    ins = three_passes(out, slot, slice(kt * P, kt * P + P), x_hi[:, kt], x_lo[:, kt],
                                       kt == 0, kt == KT - 1)
                ins.then_inc(chunk_done, 1)

            copied = [0]

            def project_tiles(part, count, x_hi, x_lo):
                for n in range(count):
                    c = START[part] + n
                    if n >= 2 or copied[0]:
                        pe.wait_ge(tile_copied, copied[0] + n - 1)
                    project(c, c % RING, bank[n % 2][:, 0:S], x_hi, x_lo)
                copied[0] += count

            def project_rows(part, x_hi, x_lo):
                pe.wait_ge(tile_copied, copied[0])
                for j in range(4):
                    c = START[part] + j
                    slot = c % RING
                    pe.wait_ge(lo_ready, c + 1)
                    for kt in (2 * j, 2 * j + 1):
                        cols = slice(kt % 2 * 512, kt % 2 * 512 + 512)
                        for t in range(TT):
                            at = slice(t * P, t * P + P)
                            nc.tensor.matmul(bank[t][:], x_hi[:, kt, at], w_hi[:, slot, cols], start=kt == 0, stop=False)
                            nc.tensor.matmul(bank[t][:], x_lo[:, kt, at], w_hi[:, slot, cols], start=False, stop=False)
                            ins = nc.tensor.matmul(bank[t][:], x_hi[:, kt, at], w_lo[:, slot, cols],
                                                   start=False, stop=kt == KT - 1)
                    ins.then_inc(chunk_done, 1)
                copied[0] += 2

            squares = [0]

            def sum_squares():
                if squares[0]:
                    pe.wait_ge(rms_ready, squares[0] // KT)
                for m in range(KT):
                    n = squares[0]
                    pe.wait_ge(sq_ready, n + 1)
                    ins = nc.tensor.matmul(bank[7][:, 0:S], ones[:], sq[:, n % 2], start=m == 0, stop=m == KT - 1)
                    ins.then_inc(sq_used, 1)
                    squares[0] += 1

            def accumulate(c, slot, x_hi, x_lo, first, last):
                pe.wait_ge(lo_ready, c + 1)
                for m in range(KT):
                    ins = three_passes(bank[m // 2][:, m % 2 * S:m % 2 * S + S], slot, slice(m * P, m * P + P),
                                       x_hi, x_lo, first and m % 2 == 0, last, skip_group_check=True)
                ins.then_inc(chunk_done, 1)

            def memory_attention(layer):
                base = layer * len(X_UNITS)

                def scores(n):
                    head, t = X_UNITS[n]
                    if base + n >= 2:
                        pe.wait_ge(x_exp, base + n - 1)
                    nc.tensor.matmul(bank[2 + n % 2][:, 0:M], xq[:, head, t * P:t * P + P], mk[:, head],
                                     start=True, stop=True).then_inc(x_score, 1)

                def turn(n):
                    pe.wait_ge(x_prob, base + n + 1)
                    if base + n >= 2:
                        pe.wait_ge(x_copied, base + n - 1)
                    for m in range(2):
                        ins = nc.tensor.transpose(bank[4 + n % 2][:, m * P:m * P + P],
                                                  prob[:, n % 2, 0, m * P:m * P + P], idt[:])
                    ins.then_inc(x_turned, 1)

                def output(n):
                    head, t = X_UNITS[n]
                    if t == 1:
                        pe.wait_ge(x_copied, base + n + 1)
                        if layer * XH + head:
                            pe.wait_ge(x_o_lo, layer * XH + head)
                        for m in range(2):
                            ins = nc.tensor.matmul(bank[6][:, 0:S], mv[:, m, head * P:head * P + P],
                                                   probT[:, head % 2, 2 * m:2 * m + 2], start=m == 0, stop=m == 1)
                        ins.then_inc(x_o, 1)

                for n in range(len(X_UNITS) + 2):
                    if n < len(X_UNITS):
                        scores(n)
                    if 1 <= n <= len(X_UNITS):
                        turn(n - 1)
                    if n >= 2:
                        output(n - 2)

            def mix_out(layer):
                base = START[f"out{layer}"]
                for kt in range(MIXT):
                    accumulate(base + kt, (base + kt) % RING, mix_hi[:, kt], mix_lo[:, kt], kt == 0, kt == MIXT - 1)

            def ffn(layer):
                base = START[f"ffn{layer}"]

                def gate_up(f, parity, c, slot):
                    if not (layer == 0 and isinstance(f, int) and f < 2):
                        pe.wait_ge(hid_ready, f + (layer * FT - 1))
                    for j in range(2):
                        project(c + j, (slot + j) % RING, bank[4 + parity][:, j * S:j * S + S], n_hi, n_lo)

                def down(f, parity, c, slot, first=False, last=False):
                    pe.wait_ge(hid_lo_ready, f + (layer * FT + 1))
                    accumulate(c, slot % RING, hid_hi[:, parity], hid_lo[:, parity], first, last)

                gate_up(0, 0, base, base)
                gate_up(1, 1, base + 2, base + 2)
                down(0, 0, base + 4, base + 4, first=True)
                with pe.Fori(0, FFN_LOOPS) as i:
                    for j in (0, 1):
                        c = base + 5 + 3 * j
                        gate_up(i * 2 + (2 + j), j, i * RING + c, c)
                        down(i * 2 + (1 + j), 1 - j, i * RING + (c + 2), c + 2)
                for f in (FT - 2, FT - 1):
                    c = base + 3 * f - 1
                    gate_up(f, f % 2, c, c)
                    down(f - 1, (f - 1) % 2, c + 2, c + 2)
                down(FT - 1, (FT - 1) % 2, base + 3 * FT - 1, base + 3 * FT - 1, last=True)

            pe.wait_ge(consts_set, 6)
            sum_squares()
            sum_squares()
            pe.wait_ge(n_lo_ready, KT)
            project_tiles("mem_k0", XH, m_hi, m_lo)
            pe.wait_ge(small_loaded, SMALL)
            nc.tensor.matmul(bank[2][0:H, :], tab[:], fwd, start=True, stop=True)
            for t in range(TT):
                for j in range(NC):
                    at = DIST0 + t * P - (CB - 1) - CS * j
                    ins = nc.tensor.matmul(bank[3][:, (t * NC + j) * H:(t * NC + j + 1) * H],
                                           fwd[:, at:at + P], tab[:], start=True, stop=True)
            ins.then_inc(table_ready, 1)
            project_rows("mem_v0", m_hi, m_lo)
            pe.wait_ge(n_lo_ready, 2 * KT)
            project_tiles("xq0", XH, n_hi, n_lo)

            def conv_tile(j, c, slot):
                project(c, slot % RING, bank[j][:, 0:S], n_hi, n_lo)
                project(c + 1, (slot + 1) % RING, bank[j][:, S:2 * S], n_hi, n_lo)
                project(c + 2, (slot + 2) % RING, bank[4 + j][:, 0:S], n_hi, n_lo)

            pe.wait_ge(tile_copied, copied[0])
            base = START["conv"]
            for j in (0, 1):
                conv_tile(j, base + 3 * j, base + 3 * j)
            with pe.Fori(1, KT // 2) as i:
                for j in (0, 1):
                    pe.wait_ge(tok_ready, i * 2 + (j - 1))
                    conv_tile(j, i * RING + (base + 3 * j), base + 3 * j)
            pe.wait_ge(tok_ready, KT)
            pe.wait_ge(table_copied, 2)
            memory_attention(0)
            pe.wait_ge(x_exp, len(X_UNITS))
            pe.wait_ge(tok_lo, KT)
            pe.wait_ge(x_o_lo, XH)
            mix_out(0)
            sum_squares()
            pe.wait_ge(n_lo_ready, 3 * KT)
            ffn(0)

            sum_squares()
            pe.wait_ge(n_lo_ready, 4 * KT)
            project_tiles("mem_k1", XH, m_hi, m_lo)
            project_rows("mem_v1", m_hi, m_lo)
            pe.wait_ge(n_lo_ready, 5 * KT)
            project_tiles("xq1", XH, n_hi, n_lo)
            pe.wait_ge(tile_copied, copied[0])
            for kv in range(2):
                for pair in range(2):
                    c = START["cmp_kv"] + 2 * kv + pair
                    if kv == 1:
                        pe.wait_ge(blocks_ready, 1)
                    project(c, c % RING, bank[pair][:, 0:S], n_hi, n_lo)
            for kv in range(2):
                pe.wait_ge(blocks_lo, kv + 1)
                for j in range(2):
                    c = START["w1_k"] + 2 * kv + j
                    pe.wait_ge(lo_ready, c + 1)
                    for l in range(8):
                        ll = 8 * j + l
                        ins = three_passes(bank[2][:, 0:G * NC], c % RING, slice(l * P, l * P + P),
                                           r_hi[:, ll].rearrange("p g c -> p (g c)"),
                                           r_lo[:, ll].rearrange("p g c -> p (g c)"), ll == 0, ll == CS - 1)
                    ins.then_inc(chunk_done, 1)
                pe.wait_ge(hmid_ready, kv + 1)
                if kv == 0:
                    nc.tensor.matmul(bank[3][:, 0:G * NC], w2[:, 0], hmid[:, 0], start=True, stop=True)\
                        .then_inc(kvc_ready, 1)
                else:
                    pe.wait_ge(kvc_copied, 1)
                    for g in range(G):
                        ins = nc.tensor.matmul(bank[3][0:NC, g * DK:(g + 1) * DK], hmid[:, 1, g * NC:(g + 1) * NC],
                                               w2[:, 1, 0:DK], start=True, stop=True)
                    ins.then_inc(kvc_ready, 1)
            pe.wait_ge(blocks_ready, 2)
            project_rows("nat_v", n_hi, n_lo)
            c = START["gates"]
            pe.wait_ge(lo_ready, c + 1)
            pe.wait_ge(kvc_copied, 1 + HPG)
            for t in range(TT):
                at, out = slice(t * P, t * P + P), bank[3][:, t * 3 * H:(t + 1) * 3 * H]
                for kt in range(KT):
                    cols = slice(kt * 3 * H, (kt + 1) * 3 * H)
                    nc.tensor.matmul(out, n_hi[:, kt, at], w_hi[:, c % RING, cols], start=kt == 0, stop=False)
                    nc.tensor.matmul(out, n_lo[:, kt, at], w_hi[:, c % RING, cols], start=False, stop=False)
                    ins = nc.tensor.matmul(out, n_hi[:, kt, at], w_lo[:, c % RING, cols], start=False, stop=kt == KT - 1)
            ins.then_inc(chunk_done, 1)
            project_tiles("k_slc", 2, n_hi, n_lo)
            project_tiles("k_win", 2, n_hi, n_lo)
            project_tiles("q", 8, n_hi, n_lo)
            pe.wait_ge(tile_copied, copied[0])
            pe.wait_ge(gate_exp, 1)
            memory_attention(1)
            pe.wait_ge(x_exp, 2 * len(X_UNITS))

            def query(g, a, t):
                return q_sb[64 * (g % 2):64 * (g % 2) + 64, 4 * (g // 2) + a, t * P:t * P + P]

            for t in range(TT):
                for g in range(G):
                    for a in range(HPG):
                        at = g // 2 * HPG + a
                        ins = nc.tensor.matmul(cmp_bank(t, g % 2)[:, at * NC:(at + 1) * NC], query(g, a, t),
                                               kc[64 * (g % 2):64 * (g % 2) + 64, g], start=True, stop=True)
                ins.then_inc(sc_ready, 1)
            pe.wait_ge(x_copied, 2 * len(X_UNITS))
            pe.wait_ge(pc_ready, TT)
            for half in range(2):
                for k in range(4):
                    g, t = divmod(4 * half + k, TT)
                    ins = nc.tensor.transpose(bank[4 + half][:, k * P:k * P + P],
                                              pc[:, t, g * HPG:(g + 1) * HPG].rearrange("p h c -> p (h c)"), idt[:])
                ins.then_inc(pcT_ready, 1)
            pe.wait_ge(pcT_copied, 2)
            pe.wait_ge(x_o_lo, 2 * XH)

            def scores(n):
                g, t, a = N_UNITS[n]
                if n >= 2:
                    pe.wait_ge(logit_ready, n - 1)
                for b in range(2):
                    ins = nc.tensor.matmul(bank[2 + n % 2][:, b * S:b * S + (t + 1) * P], query(g, a, t),
                                           ks[64 * (g % 2):64 * (g % 2) + 64, b, g // 2, 0:(t + 1) * P],
                                           start=True, stop=True)
                ins.then_inc(score, 1)

            def turn(n):
                g, t, a = N_UNITS[n]
                pe.wait_ge(prob_ready, n + 1)
                if n >= 2:
                    pe.wait_ge(probT_ready, n - 1)
                for b in range(2):
                    for kt in range(t + 1):
                        at = b * (t + 1) + kt
                        ins = nc.tensor.transpose(bank[4 + n % 2][:, at * P:at * P + P],
                                                  prob[:, n % 2, b, kt * P:kt * P + P], idt[:])
                ins.then_inc(turned, 1)

            def values(n):
                g, t, a = N_UNITS[n]
                u = g * TT + t
                if a == 0:
                    if u:
                        pe.wait_ge(o_copied, u)
                    nc.tensor.matmul(bank[6][:, 0:HPG * DK], pcT[:, u], vc[:, g], start=True, stop=False,
                                     skip_group_check=True)
                pe.wait_ge(probT_ready, n + 1)
                for b in range(2):
                    for kt in range(t + 1):
                        last = a == HPG - 1 and b == 1 and kt == t
                        ins = nc.tensor.matmul(bank[6][:, a * DK:(a + 1) * DK], probT[:, n % 2, b * (t + 1) + kt],
                                               v_nat[:, kt, b, g], start=False, stop=last, skip_group_check=True)
                ins.then_inc(pv_done, 1)

            def output(n):
                g, t, a = N_UNITS[n]
                if a == HPG - 1:
                    u = g * TT + t
                    pe.wait_ge(o_copied, u + 1)
                    if u:
                        pe.wait_ge(oT_lo, 2 * u)
                    for half in range(2):
                        ins = nc.tensor.transpose(bank[7][:, half * P:half * P + P],
                                                  o_nat[:, u % 2, half * P:half * P + P], idt[:])
                    ins.then_inc(oT_ready, 1)

            for n in range(len(N_UNITS) + 3):
                if n < len(N_UNITS):
                    scores(n)
                if 1 <= n <= len(N_UNITS):
                    turn(n - 1)
                if 2 <= n <= len(N_UNITS) + 1:
                    values(n - 2)
                if n >= 3:
                    output(n - 3)
            pe.wait_ge(oT_lo, 4 * G)
            mix_out(1)
            sum_squares()
            pe.wait_ge(n_lo_ready, 6 * KT)
            ffn(1)
            sum_squares()


def layout(x):
    def tiles(w):
        k, n = w.shape
        return w.reshape(k // P, P, n // P, P).transpose(2, 1, 0, 3).reshape(n // P, P, k)

    def rows(w):
        return w.reshape(4, 2, P, 512).transpose(0, 2, 1, 3).reshape(4, P, CHUNK)

    def by_input(w):
        return w.reshape(-1, P, CHUNK)

    conv, nsa = x["w_in_conv"][0], x["w_in_nsa"][0]
    kv0 = H * DK
    kvs = [nsa[:, kv0 + i * G * DK:kv0 + (i + 1) * G * DK] for i in range(6)]
    gates = nsa[:, kv0 + 6 * G * DK:kv0 + 6 * G * DK + 3 * H]
    q = nsa[:, :H * DK].reshape(D, G // 2, 2, HPG, DK).transpose(0, 1, 3, 2, 4).reshape(D, H * DK)
    gate_chunk = np.zeros((1, P, CHUNK), np.float32)
    gate_chunk[0, :, :KT * 3 * H] = gates.reshape(KT, P, 3 * H).transpose(1, 0, 2).reshape(P, KT * 3 * H)

    def w1(w):
        w = w.reshape(2, CS, DK, P).transpose(0, 2, 1, 3).reshape(P, 2, CHUNK)
        return w.transpose(1, 0, 2)

    def ffn(i):
        w = tiles(x["w_ffn_in"][i])
        gate, up, out = w[:FT], w[FT:], by_input(x["w_ffn_out"][i])
        parts = [gate[0], up[0]]
        for f in range(1, FT):
            parts += [gate[f], up[f], out[f - 1]]
        return np.stack(parts + [out[FT - 1]])

    b, c, u = (tiles(conv[:, i * D:(i + 1) * D]) for i in range(3))
    parts = {
        "conv": np.stack([c, u, b], 1).reshape(3 * KT, P, CHUNK),
        "xq0": tiles(conv[:, 3 * D:]), "xq1": tiles(nsa[:, -XH * P:]),
        "cmp_kv": np.concatenate([tiles(kvs[0]), tiles(kvs[1])]),
        "w1_k": w1(x["cmp_w1_k"][0]), "w1_v": w1(x["cmp_w1_v"][0]),
        "nat_v": rows(np.concatenate([kvs[3], kvs[5]], 1)), "gates": gate_chunk,
        "k_slc": tiles(kvs[2]), "k_win": tiles(kvs[4]), "q": tiles(q),
    }
    for i in range(2):
        parts[f"mem_k{i}"] = tiles(x["w_mem_kv"][i][:, :XH * P])
        parts[f"mem_v{i}"] = rows(x["w_mem_kv"][i][:, XH * P:])
        parts[f"out{i}"] = by_input(x["w_out"][i])
        parts[f"ffn{i}"] = ffn(i)
    for name, count in PARTS:
        assert parts[name].shape == (count, P, CHUNK), name

    def features(a):
        return a.reshape(-1, KT, P).transpose(2, 1, 0)

    gains = np.stack([x["norm_mem_g"][0], x["norm_mix_g"][0], x["norm_ffn_g"][0],
                      x["norm_mem_g"][1], x["norm_mix_g"][1], x["norm_ffn_g"][1], x["norm_final_g"]])

    def positions(p):
        return p.reshape(2, CS, DK).transpose(0, 2, 1).reshape(P, CS)

    dist = np.arange(-DIST0, DIST0)
    near = BUCKETS // 2
    far = near + (np.log(np.maximum(dist, 1).astype(np.float32) / np.float32(near))
                  / np.float32(np.log(128 / near)) * (BUCKETS - near)).astype(np.int32)
    bucket = np.where(dist < 0, BUCKETS, np.where(dist < near, dist, np.minimum(far, BUCKETS - 1)))
    forward = (np.arange(BUCKETS + 1)[:, None] == bucket).astype(np.float32)
    return {
        "stream": np.concatenate([parts[name] for name, _ in PARTS]),
        "xT": features(x["x"][0]), "memT": features(x["mem"][0]),
        "gains": features(gains).transpose(0, 2, 1),
        "conv_w": features(x["conv_w"][0]).transpose(0, 2, 1),
        "cmp_pos": np.stack([positions(x["cmp_pos_k"][0]), positions(x["cmp_pos_v"][0])], 1),
        "cmp_w2": np.stack([np.concatenate([w[0], w[0]], 1) for w in (x["cmp_w2_k"], x["cmp_w2_v"])], 1),
        "rel_bias": x["rel_bias"], "dist_fwd": forward,
        "ident": np.eye(P, dtype=np.float32),
    }


def kernel(**inputs):
    import concourse.bacc as bacc
    from concourse.bass_utils import run_bass_kernel_spmd

    arrays = layout({k: np.asarray(v) for k, v in inputs.items()})
    arrays = {k: np.ascontiguousarray(v) for k, v in arrays.items()}
    nc = bacc.Bacc("TRN2", target_bir_lowering=False, num_devices=1)
    args = {k: nc.dram_tensor(k, a.shape, mybir.dt.from_np(a.dtype), kind="ExternalInput").ap()
            for k, a in arrays.items()}
    outT = nc.dram_tensor("outT", (P, KT, S), F32, kind="ExternalOutput").ap()
    build(nc, outT=outT, **args)
    got = run_bass_kernel_spmd(nc, [arrays], core_ids=[0]).results[0]["outT"]
    return np.ascontiguousarray(np.asarray(got).transpose(2, 1, 0).reshape(1, S, D))
```

```python
from contextlib import ExitStack

import numpy as np

import concourse.bass as bass
from concourse import mybir

ALU = mybir.AluOpType
ACT = mybir.ActivationFunctionType
AX_X = mybir.AxisListType.X
F32 = mybir.dt.float32
F32R = mybir.dt.float32r

P = 128
D, S, M = 1024, 256, 256
KT = D // P
TT = S // P
XH = 4
H, G, HPG, DK = 16, 4, 4, 64
MIXT = (D + XH * P) // P
FT = 2816 // P
CB, CS = 32, 16
NC = (S - CB) // CS + 1
BUCKETS = 32
CHUNK = 8 * P
RING = 6
RAW = RING // 2
AHEAD = 5
EPS = 1e-6
NEG = -1e30
FFN_LOOPS = (FT - 4) // 2
CONSTS = 7
SMALL = 16 * 6
XSCALE = float(P) ** -0.5
SCALE = float(DK) ** -0.5
DIST0 = S

PARTS = [("mem_k0", 4), ("mem_v0", 4), ("xq0", 4), ("conv", 3 * KT), ("out0", MIXT), ("ffn0", 3 * FT - 1),
         ("mem_k1", 5), ("mem_v1", 4), ("cmp_k", 2), ("kq0", 3), ("w1_k", 2), ("cmp_v", 2), ("q0", 3), ("w1_v", 2),
         ("gates", 1), ("nat_v", 4), ("kq1", 6), ("xq1", 4), ("out1", MIXT), ("ffn1", 3 * FT)]
START, TOTAL = {}, 0
for _name, _count in PARTS:
    START[_name] = TOTAL
    TOTAL += _count
COUNT = dict(PARTS)
LAST_DOWN = [START["mem_k1"] + 2, START["ffn1"] + 3 * FT - 1]
KEY_CHUNKS = [[START["mem_k0"] + a for a in range(XH)], [START["mem_k1"] + a for a in (0, 1, 3, 4)]]

MEM_UNITS = [("mem", a, t) for a in range(XH) for t in range(TT)]
NSA_UNITS = [[("nsa", g, t, a) for t in range(TT) for a in range(HPG)] for g in range(G)]
UNITS = MEM_UNITS + NSA_UNITS[0] + NSA_UNITS[1] + MEM_UNITS + NSA_UNITS[2] + NSA_UNITS[3]
FIRST_UNIT = [0, len(MEM_UNITS), len(UNITS)]
DRAIN = 5

OUT_ORDER = [list(range(MIXT)), [0, 1, 2, 3, 8, 9, 10, 11, 4, 5, 6, 7]]


def halves(items, starts):
    return [(r + half, item + (half,)) for item, r in zip(items, starts) for half in range(2)]


def by_step(pairs):
    return {r: [item for at, item in pairs if at == r] for r, _ in pairs}


BESIDE = [
    by_step([(r, ("out", j, half)) for j, r in enumerate([*range(KT), 9, 11, 12]) for half in range(2)]),
    by_step([(0, ("cmp_scores", 0)), (2, ("cmp_turn", 0)), (13, ("cmp_scores", 1)), (15, ("cmp_turn", 1))]
            + halves([("tile", "kq1", j) for j in range(6)], range(0, 12, 2))
            + halves([("tile", "xq1", j) for j in range(XH)], range(12, 20, 2))
            + halves([("out", j) for j in range(10)], [*range(20, 36, 2), 37, 39])),
]


def steps_of(layer):
    first, end = FIRST_UNIT[layer], FIRST_UNIT[layer + 1]
    return [(n, BESIDE[layer].get(n - first, [])) for n in range(first, end + DRAIN)]


def is_unit(layer, n):
    return FIRST_UNIT[layer] <= n < FIRST_UNIT[layer + 1]


def makes_output(n):
    return UNITS[n][2] == TT - 1 if UNITS[n][0] == "mem" else UNITS[n][3] == HPG - 1


def outputs_before(n, kind=None):
    return sum(makes_output(m) and kind in (None, UNITS[m][0]) for m in range(n))


def values_through(n):
    return sum(UNITS[m][0] == "nsa" or makes_output(m) for m in range(n + 1))


def keys_of(n):
    return TT if UNITS[n][0] == "mem" else 2 * (UNITS[n][2] + 1)


def build(nc, stream, xT, memT, gains, conv_w, cmp_pos, cmp_w2, rel_bias, dist_fwd, ident, outT):
    table_dram = nc.dram_tensor("bias_by_distance", (H, 2 * S), F32, kind="Internal").ap()
    with ExitStack() as ctx:
        def sb(name, shape, dt=F32):
            return ctx.enter_context(nc.sbuf_tensor(name, shape, dt))

        def sem(name):
            return ctx.enter_context(nc.semaphore(name))

        raw = sb("raw", [P, RAW, CHUNK])
        w_hi = sb("w_hi", [P, RING, CHUNK], F32R)
        w_lo = sb("w_lo", [P, RING, CHUNK], F32R)
        h = sb("h", [P, KT, S])
        mem = sb("mem", [P, KT, M])
        n_hi = sb("n_hi", [P, KT, S], F32R)
        n_lo = sb("n_lo", [P, KT, S], F32R)
        mix_hi = sb("mix_hi", [P, MIXT, S], F32R)
        mix_lo = sb("mix_lo", [P, MIXT, S], F32R)
        m_hi, m_lo = mix_hi[:, 0:KT], mix_lo[:, 0:KT]
        sq_sum = sb("sq_sum", [P, 2, S])
        rms = sb("rms", [P, S])
        rstd = sb("rstd", [P, S])
        mem_rstd = sb("mem_rstd", [P, M])
        mem_rcol = sb("mem_rcol", [P, TT])
        normed = sb("normed", [P, 2, S])
        gain = sb("gain", [P, 7, KT])
        taps = sb("taps", [P, 3, KT])
        ones = sb("ones", [P, P])
        idt = sb("idt", [P, P])
        eps = sb("eps", [P, 1])
        warm = sb("warm", [P, 1])
        tab = sb("tab", [BUCKETS + 1, H])
        bias = sb("bias", [P, H, S])
        bias_c = sb("bias_c", [P, TT, H, NC])
        pos = sb("pos", [P, 2, CS])
        w2 = sb("w2", [P, 2, P])
        xq = sb("xq", [P, XH, S])
        mk = sb("mk", [P, XH, M])
        mv = sb("mv", [P, 2, XH * P])
        silu = sb("silu", [P, 2, S])
        hid = sb("hid", [P, 2, S])
        hid_hi = sb("hid_hi", [P, 2, S], F32R)
        hid_lo = sb("hid_lo", [P, 2, S], F32R)
        sq = [silu, hid]
        q_sb = mem
        ks = sb("ks", [P, 2, 2, S])
        v_nat = sb("v_nat", [P, TT, 2, G, DK])
        gate = sb("gate", [P, TT, 3, H])
        c_sb = v_nat[:, 0].rearrange("p b g d -> p b (g d)")
        conv = v_nat[:, 1].rearrange("p b g d -> p b (g d)")
        vpad = ks[:].rearrange("p b a s -> p (b a s)")[:, 0:2 * (S + 2)].rearrange("p (b s) -> p b s", b=2)
        r_hi = sb("r_hi", [P, CS, G, NC], F32R)
        r_lo = sb("r_lo", [P, CS, G, NC], F32R)
        hmid = sb("hmid", [P, 2, G * NC])
        kc = sb("kc", [P, G, NC])
        vc = sb("vc", [P, G, HPG * DK])
        lc = sb("lc", [P, H, NC])
        pc = sb("pc", [P, H, 32])
        pcT = sb("pcT", [P, G * TT, P])
        att = sb("att", [P, 3, 2, S])
        probT = sb("probT", [P, 2, 4, P])
        xprobT = sb("xprobT", [P, 2, TT, P])
        fwd = att[0:BUCKETS + 1, 1].rearrange("p b s -> p (b s)")
        tab_row = att[0:H, 2].rearrange("p b s -> p (b s)")
        r_raw = att[:].rearrange("p a b s -> p (a b s)")[:, 0:CS * G * NC]\
            .rearrange("p (l g c) -> p l g c", l=CS, g=G)
        col = sb("col", [P, 3, 5, 2])
        colc = sb("colc", [P, 4, H])

        bank = [ctx.enter_context(nc.psum_tensor(f"bank{i}", [P, 512], F32)) for i in range(8)]

        raw_loaded = [sem(f"raw_loaded{i}") for i in range(RAW)]
        hi_ready = sem("hi_ready")
        lo_ready = sem("lo_ready")
        chunk_done = sem("chunk_done")
        gain_loaded = sem("gain_loaded")
        x_loaded = sem("x_loaded")
        mem_loaded = [sem(f"mem_loaded{i}") for i in range(2)]
        small_loaded = sem("small_loaded")
        consts_set = sem("consts_set")
        table_ready = sem("table_ready")
        table_copied = sem("table_copied")
        table_stored = sem("table_stored")
        bias_loaded = sem("bias_loaded")
        dve_step = sem("dve_step")
        out_gained = sem("out_gained")
        out_ready = sem("out_ready")
        pool_out_ready = sem("pool_out_ready")
        out_stored = sem("out_stored")

        NORMS = ["mem0", "x0", "f0", "mem1", "x1", "f1", "end"]
        sq_ready = sem("sq_ready")
        sq_added = sem("sq_added")
        sum_ready = sem("sum_ready")
        rms_ready = sem("rms_ready")
        rstd_ready = sem("rstd_ready")
        normed_ready = sem("normed_ready")
        n_hi_ready = sem("n_hi_ready")
        n_lo_ready = sem("n_lo_ready")
        bank_done = sem("bank_done")
        residual_added = sem("residual_added")
        rcol_ready = sem("rcol_ready")
        rcol_copied = sem("rcol_copied")
        mk_copied = sem("mk_copied")

        tile_copied = sem("tile_copied")
        c_copied = sem("c_copied")
        tok_ready = sem("tok_ready")
        tok_hi = sem("tok_hi")
        tok_lo = sem("tok_lo")
        gate_scaled = sem("gate_scaled")
        up_scaled = sem("up_scaled")
        silu_ready = sem("silu_ready")
        hid_ready = sem("hid_ready")
        hid_hi_ready = sem("hid_hi_ready")
        hid_lo_ready = sem("hid_lo_ready")
        blocks_ready = sem("blocks_ready")
        blocks_hi = sem("blocks_hi")
        blocks_lo = sem("blocks_lo")
        hmid_ready = sem("hmid_ready")
        kvc_ready = sem("kvc_ready")
        kvc_copied = sem("kvc_copied")
        gate_exp = sem("gate_exp")
        sc_ready = sem("sc_ready")
        lc_ready = sem("lc_ready")
        lc_exp = sem("lc_exp")
        pc_ready = sem("pc_ready")
        pcT_ready = sem("pcT_ready")
        pcT_copied = sem("pcT_copied")
        scores_ready = sem("scores_ready")
        max_ready = sem("max_ready")
        exp_ready = sem("exp_ready")
        prob_ready = sem("prob_ready")
        turned = sem("turned")
        probT_ready = sem("probT_ready")
        values_done = sem("values_done")
        out_hi = sem("out_hi")
        out_lo = sem("out_lo")

        def f32(ap):
            return ap.bitcast(F32)

        DVE_PAIRS = 3
        SUMMED = ["mem0", "x0", "f0", "x1", "f1", "end"]
        ADDS = KT // 2

        def norm_source(name):
            return mem if name.startswith("mem") else h

        def cmp_bank(odd):
            return bank[2 + odd]

        def tile_target(part, j):
            if part.startswith("xq"):
                return xq[:, j], XSCALE
            if part == "q0":
                return q_sb[:, 1 + j], SCALE
            pair = int(part[-1])
            return (ks[:, j, pair], 1.0) if j < 2 else (q_sb[:, 4 * pair + j - 2], SCALE)

        def output_of(n, mix):
            u = UNITS[n]
            return mix[:, KT + u[1]] if u[0] == "mem" else mix[:, 2 * u[1]:2 * u[1] + 2, u[2] * P:u[2] * P + P]

        def output_psum(n):
            return bank[7][:, 0:S] if UNITS[n][0] == "mem" else bank[7][:, 0:S].rearrange("p (h q) -> p h q", h=2)

        block = ctx.enter_context(nc.Block())

        @block.sync
        def _(sp):
            def load(c, slot):
                sp.dma_start(raw[:, slot], stream[c]).then_inc(raw_loaded[slot], 16)

            load(0, 0)
            sp.dma_start(gain[:], gains).then_inc(gain_loaded, 16)
            for i in range(2):
                half = slice(i * KT // 2, (i + 1) * KT // 2)
                sp.dma_start(mem[:, half], memT[:, half]).then_inc(mem_loaded[i], 16)
            load(1, 1)
            sp.dma_start(h[:], xT).then_inc(x_loaded, 16)
            load(2, 2)
            full = TOTAL // RAW
            with sp.Fori(1, full) as i:
                for slot in range(RAW):
                    sp.wait_ge(lo_ready, i * RAW + (slot + 1 - RAW))
                    load(i * RAW + slot, slot)
            for c in range(full * RAW, TOTAL):
                sp.wait_ge(lo_ready, c - RAW + 1)
                load(c, c % RAW)
            for n in range(DVE_PAIRS):
                sp.wait_ge(out_ready, n + 1)
                sp.dma_start(outT[:, 2 * n:2 * n + 2], mem[:, 2 * n:2 * n + 2]).then_inc(out_stored, 16)
            sp.wait_ge(pool_out_ready, 1)
            sp.dma_start(outT[:, 2 * DVE_PAIRS:KT], mem[:, 2 * DVE_PAIRS:KT]).then_inc(out_stored, 16)
            sp.wait_ge(out_stored, 16 * (DVE_PAIRS + 1))

        @block.gpsimd
        def _(pool):
            for n, (tile, value) in enumerate(((ones, 1.0), (eps, EPS), (vpad, 0.0),
                                               (bias_c, NEG), (tab[BUCKETS:BUCKETS + 1, :], NEG), (pc, 0.0),
                                               (vc, 0.0))):
                if n:
                    pool.wait_ge(consts_set, n)
                nc.gpsimd.memset(tile if tile.shape[0] == 1 else tile[:], value).then_inc(consts_set, 1)
                if n == 1:
                    for small, src in ((tab[0:BUCKETS, :], rel_bias), (fwd, dist_fwd), (idt[:], ident),
                                       (taps[:], conv_w), (pos[:], cmp_pos), (w2[:], cmp_w2)):
                        pool.dma_start(small, src).then_inc(small_loaded, 16)
            pool.wait_ge(table_copied, 1)
            pool.dma_start(table_dram, tab_row).then_inc(table_stored, 16)
            pool.wait_ge(table_stored, 16)
            pool.wait_ge(chunk_done, START["conv"])
            rows = bass.AP(tensor=table_dram.tensor, offset=DIST0 - (P - 1), ap=[[1, P], [2 * S, H], [1, S]])
            pool.dma_start(bias[:], rows).then_inc(bias_loaded, 16)
            pool.wait_ge(bias_loaded, 16)
            pool.wait_ge(out_gained, KT)
            pool.wait_ge(rstd_ready, len(SUMMED))
            rest = mem[:, 2 * DVE_PAIRS:KT]
            nc.gpsimd.tensor_tensor(rest, rest, rstd[:, None].to_broadcast([P, KT - 2 * DVE_PAIRS, S]), ALU.mult)\
                .then_inc(pool_out_ready, 1)

        @block.scalar
        def _(act):
            split = [0]

            def split_hi(c, slot, landed, may_wait=True):
                act.wait_ge(raw_loaded[slot % RAW], landed)
                if may_wait:
                    act.wait_ge(chunk_done, c - RING + 1)
                nc.scalar.copy(w_hi[:, slot], raw[:, slot % RAW]).then_inc(hi_ready, 1)

            def split_to(end):
                while split[0] < min(end, TOTAL):
                    c = split[0]
                    split_hi(c, c % RING, 16 * (c // RAW + 1), c >= RING)
                    split[0] += 1

            def split_loop(i, k, count):
                for _ in range(count):
                    c = split[0] + k[0]
                    split_hi(i * RING + c, c % RING, i * (16 * RING // RAW) + 16 * (c // RAW + 1))
                    k[0] += 1

            tiles = [0]

            def copy_tile(c, out, scale=1.0):
                act.wait_ge(chunk_done, c + 1)
                nc.scalar.mul(out, bank[tiles[0] % 2][:, 0:S], scale).then_inc(tile_copied, 1)
                tiles[0] += 1

            def copy_tiles(part, targets):
                for n, target in enumerate(targets):
                    split_to(START[part] + n + 1 + AHEAD)
                    copy_tile(START[part] + n, *target)

            def copy_rows(part, outs, factors=(1.0, 1.0)):
                split_to(START[part] + 4 + AHEAD)
                act.wait_ge(chunk_done, START[part] + 4)
                for t, out in enumerate(outs):
                    nc.scalar.mul(out, bank[t][:], factors[t]).then_inc(tile_copied, 1)

            squares = [0]
            his = [0]
            normed_tiles = [0]

            def gained(name):
                src, hi = (mem, m_hi) if name.startswith("mem") else (h, n_hi)
                act.wait_ge(gain_loaded, 16)
                for m in range(KT):
                    if name == "mem0":
                        act.wait_ge(mem_loaded[m // (KT // 2)], 16)
                    elif name != "mem1":
                        act.wait_ge(residual_added, KT // 2 * (SUMMED.index(name) - 2) + m // 2 + 1)
                    nc.scalar.mul(hi[:, m], src[:, m], gain[:, NORMS.index(name), m:m + 1]).then_inc(n_hi_ready, 1)
                    his[0] += 1

            def square(name):
                src, k = norm_source(name), SUMMED.index(name)
                for m in range(KT // 2):
                    if name == "mem0":
                        act.wait_ge(mem_loaded[1], 16)
                    elif name == "x0":
                        act.wait_ge(x_loaded, 16)
                    else:
                        act.wait_ge(residual_added, KT // 2 * (k - 2) + m + 1)
                    if m >= 2:
                        act.wait_ge(sq_added, ADDS * k + 1)
                    elif k:
                        act.wait_ge(sq_added, ADDS * (k - 1) + 2 + m)
                    nc.scalar.activation(sq[m % 2][:], src[:, 2 * m:2 * m + 2], ACT.Square).then_inc(sq_ready, 1)

            def root(name):
                k = SUMMED.index(name)
                act.wait_ge(sum_ready, k + 1)
                if k:
                    act.wait_ge(rstd_ready, k)
                act.wait_ge(consts_set, CONSTS)
                nc.scalar.activation(rms[:], bank[7][:, 0:S], ACT.Sqrt, bias=eps[:, 0:1],
                                     scale=1.0 / D).then_inc(rms_ready, 1)

            def norm_hi():
                for m in range(KT):
                    act.wait_ge(normed_ready, normed_tiles[0] + 1)
                    nc.scalar.copy(n_hi[:, m], normed[:, normed_tiles[0] % 2]).then_inc(n_hi_ready, 1)
                    normed_tiles[0] += 1
                    if m % 2:
                        split_to(split[0] + 1)

            def exp(n):
                u, k, b = UNITS[n], n % 3, bank[4 + n % 2]
                act.wait_ge(max_ready, n + 1)
                if u[0] == "mem":
                    nc.scalar.activation(att[:, k, 0], b[:, 0:M], ACT.Exp, bias=col[:, k, 0, 0:1],
                                         accum_out=col[:, k, 2, 0:1]).then_inc(exp_ready, 1)
                    return
                keys = (u[2] + 1) * P
                for br in range(2):
                    ins = nc.scalar.activation(att[:, k, br, 0:keys], att[:, k, br, 0:keys], ACT.Exp,
                                               bias=col[:, k, 0, br:br + 1], accum_out=col[:, k, 2, br:br + 1])
                ins.then_inc(exp_ready, 1)

            def copy_turned(n):
                u = UNITS[n]
                act.wait_ge(turned, n + 1)
                if u[0] == "mem":
                    if u[2] == 0 and outputs_before(n, "mem"):
                        last = max(m for m in range(n) if UNITS[m][0] == "mem")
                        act.wait_ge(values_done, values_through(last))
                    out, blocks = xprobT[:, :, u[2]], TT
                else:
                    before = [m for m in range(n) if UNITS[m][0] == "nsa" and m % 2 == n % 2]
                    if before:
                        act.wait_ge(values_done, values_through(before[-1]))
                    blocks = keys_of(n)
                    out = probT[:, n % 2, 0:blocks]
                nc.scalar.copy(out, bank[6][:, 0:blocks * P].rearrange("p (b q) -> p b q", q=P)).then_inc(probT_ready, 1)

            def output_hi(n):
                if not makes_output(n):
                    return
                u = UNITS[n]
                act.wait_ge(values_done, values_through(n))
                nc.scalar.copy(output_of(n, mix_hi), output_psum(n)).then_inc(out_hi, 1)

            def attention(layer):
                chunk = START["out0"] if layer == 0 else START["kq1"]
                for n, beside in steps_of(layer):
                    split_to(chunk + AHEAD)
                    if is_unit(layer, n - 3):
                        copy_turned(n - 3)
                    if is_unit(layer, n):
                        exp(n)
                    if is_unit(layer, n - 4):
                        output_hi(n - 4)
                    for what, *which in beside:
                        if what == "tile" and which[-1]:
                            copy_tile(chunk, *tile_target(*which[:-1]))
                        elif what == "cmp_scores":
                            act.wait_ge(lc_ready, which[0] + 1)
                            nc.scalar.activation(lc[:], lc[:], ACT.Exp).then_inc(lc_exp, 1)
                        chunk += what in ("tile", "out") and which[-1]

            def ffn(layer):
                base = START[f"ffn{layer}"]

                def gate_silu(f, parity):
                    act.wait_ge(gate_scaled, f + (layer * FT + 1))
                    nc.scalar.activation(silu[:, parity], silu[:, parity], ACT.Silu).then_inc(silu_ready, 1)

                def hidden_hi(f, parity):
                    act.wait_ge(hid_ready, f + (layer * FT + 1))
                    nc.scalar.copy(hid_hi[:, parity], hid[:, parity]).then_inc(hid_hi_ready, 1)

                gained(f"f{layer}")
                square(f"f{layer}")
                split_to(base + 1 + AHEAD)
                root(f"f{layer}")
                split_to(base + 2 + AHEAD)
                gate_silu(0, 0)
                hidden_hi(0, 0)
                split_to(base + 4 + AHEAD)
                gate_silu(1, 1)
                hidden_hi(1, 1)
                if layer == 0:
                    gained("mem1")
                split_to(base + 5 + AHEAD)
                with act.Fori(0, FFN_LOOPS) as i:
                    k = [0]
                    for j in (0, 1):
                        split_loop(i, k, 1)
                        gate_silu(i * 2 + (2 + j), j)
                        split_loop(i, k, 1)
                        hidden_hi(i * 2 + (2 + j), j)
                        split_loop(i, k, 1)
                split[0] += FFN_LOOPS * RING
                for f in (FT - 2, FT - 1):
                    split_to(base + 3 * f + 1 + AHEAD)
                    gate_silu(f, f % 2)
                    hidden_hi(f, f % 2)

            act.wait_ge(consts_set, 2)
            nc.scalar.activation(warm[:], eps[:], ACT.Sqrt)
            split_to(1)
            gained("mem0")
            split_to(2)
            square("mem0")
            split_to(3)
            square("x0")
            root("mem0")
            split_to(4)
            root("x0")
            norm_hi()
            split_to(START["xq0"] + AHEAD)
            act.wait_ge(rcol_ready, 1)
            nc.scalar.copy(mem_rcol[:], bank[6][:, 0:TT]).then_inc(rcol_copied, 1)
            act.wait_ge(rcol_copied, 1)
            mem_factors = [mem_rcol[:, t:t + 1] for t in range(TT)]
            copy_rows("mem_v0", [mv[:, t] for t in range(2)], mem_factors)
            copy_tiles("xq0", [tile_target("xq0", n) for n in range(XH)])

            split_to(START["conv"] + AHEAD)
            with act.Fori(0, KT // 2) as i:
                k = [0]
                for j in (0, 1):
                    split_loop(i, k, 2)
                    act.wait_ge(chunk_done, i * RING + (START["conv"] + 3 * j + 2))
                    nc.scalar.copy(c_sb[:, j], bank[j][:, 0:S]).then_inc(c_copied, 1)
                    split_loop(i, k, 1)
                    act.wait_ge(tok_ready, i * 2 + (j + 1))
                    nc.scalar.copy(mix_hi[:, bass.ds(i * 2 + j, 1)], conv[:, j:j + 1]).then_inc(tok_hi, 1)
            split[0] += 3 * KT
            act.wait_ge(table_stored, 16)
            attention(0)
            split_to(START["ffn0"] + AHEAD)
            ffn(0)

            square("x1")
            split_to(KEY_CHUNKS[1][2] + 1 + AHEAD)
            root("x1")
            norm_hi()
            copy_rows("mem_v1", [mv[:, t] for t in range(2)], mem_factors)
            for kv, (raws, w1, tiles_part) in enumerate((("cmp_k", "w1_k", "kq0"), ("cmp_v", "w1_v", "q0"))):
                split_to(START[raws] + 2 + AHEAD)
                act.wait_ge(blocks_ready, kv + 1)
                nc.scalar.copy(r_hi[:], r_raw[:]).then_inc(blocks_hi, 1)
                copy_tiles(tiles_part, [tile_target(tiles_part, j) for j in range(3)])
                split_to(START[w1] + 2 + AHEAD)
                act.wait_ge(chunk_done, START[w1] + 2)
                nc.scalar.activation(hmid[:, kv], bank[4][:, 0:G * NC], ACT.Silu).then_inc(hmid_ready, 1)
            split_to(START["gates"] + 1 + AHEAD)
            act.wait_ge(chunk_done, START["gates"] + 1)
            nc.scalar.activation(gate[:].rearrange("p t b h -> p (t b h)"), bank[6][:, 0:TT * 3 * H],
                                 ACT.Exp, scale=-1.0).then_inc(gate_exp, 1)
            copy_rows("nat_v", [v_nat[:, t].rearrange("p b g d -> p (b g d)") for t in range(TT)])
            attention(1)
            split_to(START["ffn1"] + AHEAD)
            ffn(1)
            square("end")
            for m in range(KT):
                nc.scalar.mul(mem[:, m], h[:, m], gain[:, NORMS.index("end"), m:m + 1]).then_inc(out_gained, 1)
                if m == 3:
                    root("end")

        @block.vector
        def _(dve):
            split = [0]
            steps = [0]

            def link(ins):
                steps[0] += 1
                ins.then_inc(dve_step, 1)
                dve.wait_ge(dve_step, steps[0])

            def split_lo(c, slot):
                dve.wait_ge(hi_ready, c + 1)
                nc.vector.tensor_tensor(w_lo[:, slot], raw[:, slot % RAW], f32(w_hi[:, slot]), ALU.subtract)\
                    .then_inc(lo_ready, 1)

            def split_to(end):
                while split[0] < min(end, TOTAL):
                    split_lo(split[0], split[0] % RING)
                    split[0] += 1

            def split_loop(i, k, count):
                for _ in range(count):
                    c = split[0] + k[0]
                    split_lo(i * RING + c, c % RING)
                    k[0] += 1

            his = [0]
            normed_tiles = [0]
            residuals = [0]

            def add_residual(done, b):
                if b < 3:
                    dve.wait_ge(bank_done, residuals[0] // 4 * 3 + b + 1)
                else:
                    dve.wait_ge(chunk_done, done)
                hh = h[:, 2 * b:2 * b + 2]
                nc.vector.tensor_tensor(hh, bank[b][:].rearrange("p (m s) -> p m s", m=2), hh, ALU.add)\
                    .then_inc(residual_added, 1)
                residuals[0] += 1

            def gained_lo(name, m):
                src, hi, lo = (mem, m_hi, m_lo) if name.startswith("mem") else (h, n_hi, n_lo)
                dve.wait_ge(gain_loaded, 16)
                if name != "mem0" and name != "mem1":
                    dve.wait_ge(residual_added, KT // 2 * (SUMMED.index(name) - 2) + m // 2 + 1)
                dve.wait_ge(n_hi_ready, his[0] + 1)
                nc.vector.scalar_tensor_tensor(out=lo[:, m], in0=src[:, m],
                                               scalar=gain[:, NORMS.index(name), m:m + 1], in1=f32(hi[:, m]),
                                               op0=ALU.mult, op1=ALU.subtract).then_inc(n_lo_ready, 1)
                his[0] += 1

            def add_squares(name):
                k = SUMMED.index(name)
                dve.wait_ge(sq_ready, KT // 2 * k + 2)
                if k:
                    dve.wait_ge(sum_ready, k)
                nc.vector.tensor_tensor(sq_sum[:], sq[0][:], sq[1][:], ALU.add).then_inc(sq_added, 1)
                for m in (2, 3):
                    dve.wait_ge(sq_ready, KT // 2 * k + m + 1)
                    dve.wait_ge(sq_added, ADDS * k + m - 1)
                    nc.vector.tensor_tensor(sq_sum[:], sq_sum[:], sq[m % 2][:], ALU.add).then_inc(sq_added, 1)
                dve.wait_ge(sq_added, ADDS * k + 3)
                nc.vector.tensor_tensor(sq_sum[:, 0], sq_sum[:, 0], sq_sum[:, 1], ALU.add).then_inc(sq_added, 1)

            def inverse(name):
                k = SUMMED.index(name)
                dve.wait_ge(rms_ready, k + 1)
                nc.vector.reciprocal((mem_rstd if name == "mem0" else rstd)[:], rms[:]).then_inc(rstd_ready, 1)
                dve.wait_ge(rstd_ready, k + 1)

            def norm(name):
                gcol = NORMS.index(name)

                def low(m, n):
                    dve.wait_ge(n_hi_ready, his[0] + 1)
                    nc.vector.tensor_tensor(n_lo[:, m], normed[:, n % 2], f32(n_hi[:, m]), ALU.subtract)\
                        .then_inc(n_lo_ready, 1)
                    his[0] += 1

                for m in range(KT):
                    n = normed_tiles[0]
                    if n >= 2:
                        dve.wait_ge(n_lo_ready, his[0])
                    nc.vector.scalar_tensor_tensor(out=normed[:, n % 2], in0=h[:, m], scalar=gain[:, gcol, m:m + 1],
                                                   in1=rstd[:], op0=ALU.mult, op1=ALU.mult).then_inc(normed_ready, 1)
                    if m >= 1:
                        low(m - 1, n - 1)
                    if m % 2:
                        split_to(split[0] + 1)
                    normed_tiles[0] += 1
                low(KT - 1, normed_tiles[0] - 1)

            def memory_keys(layer, pair):
                dve.wait_ge(chunk_done, KEY_CHUNKS[layer][2 * pair + 1] + 1)
                nc.vector.tensor_tensor(mk[:, 2 * pair:2 * pair + 2], bank[4 + pair][:].rearrange("p (a m) -> p a m", a=2),
                                        mem_rstd[:, None].to_broadcast([P, 2, M]), ALU.mult).then_inc(mk_copied, 1)

            def largest(n):
                u, k, b = UNITS[n], n % 3, bank[4 + n % 2]
                dve.wait_ge(scores_ready, n + 1)
                if u[0] == "mem":
                    if n >= 3:
                        dve.wait_ge(turned, n - 2)
                    nc.vector.reduce_max(col[:, k, 0, 0:1], b[:, 0:M], AX_X, negate=True).then_inc(max_ready, 1)
                    return
                keys, head = (u[2] + 1) * P, u[1] * HPG + u[3]
                dve.wait_ge(turned, n - 2)
                link(nc.vector.tensor_tensor(att[:, k, :, 0:keys], b[:].rearrange("p (b s) -> p b s", b=2)[:, :, 0:keys],
                                             bias[:, head, None, keys - 1::-1].to_broadcast([P, 2, keys]), ALU.add))
                nc.vector.reduce_max(col[:, k, 0], att[:, k, :, 0:keys], AX_X, negate=True).then_inc(max_ready, 1)

            def scale(n):
                u, k = UNITS[n], n % 3
                dve.wait_ge(exp_ready, n + 1)
                if u[0] == "mem":
                    link(nc.vector.reciprocal(col[:, k, 3, 0:1], col[:, k, 2, 0:1]))
                    nc.vector.tensor_scalar(att[:, k, 0], att[:, k, 0], col[:, k, 3, 0:1], None, ALU.mult)\
                        .then_inc(prob_ready, 1)
                    return
                keys, head = (u[2] + 1) * P, u[1] * HPG + u[3]
                link(nc.vector.reciprocal(col[:, k, 3], col[:, k, 2]))
                link(nc.vector.tensor_tensor(col[:, k, 4], col[:, k, 3], gate[:, u[2], 1:3, head], ALU.mult))
                for br in range(2):
                    ins = nc.vector.tensor_scalar(att[:, k, br, 0:keys], att[:, k, br, 0:keys],
                                                  col[:, k, 4, br:br + 1], None, ALU.mult)
                ins.then_inc(prob_ready, 1)

            def output_lo(n):
                if not makes_output(n):
                    return
                dve.wait_ge(out_hi, outputs_before(n) + 1)
                nc.vector.tensor_tensor(output_of(n, mix_lo), output_psum(n), f32(output_of(n, mix_hi)),
                                        ALU.subtract).then_inc(out_lo, 1)

            def compressed(pair):
                dve.wait_ge(sc_ready, pair + 1)
                if pair:
                    dve.wait_ge(pc_ready, pair)
                    dve.wait_ge(pcT_ready, pair)
                heads = slice(2 * HPG * pair, 2 * HPG * (pair + 1))
                lcs = lc[:].rearrange("p (t o a) c -> p t o (a c)", t=TT, o=2)
                biases = bias_c[:, :, heads].rearrange("p t (o a) c -> p t o (a c)", o=2)
                for odd in range(2):
                    ins = nc.vector.tensor_tensor(lcs[:, :, odd], cmp_bank(odd)[:, 0:TT * HPG * NC].rearrange(
                        "p (t x) -> p t x", t=TT), biases[:, :, odd], ALU.add)
                link(ins)
                link(nc.vector.reduce_max(colc[:, 0], lc[:], AX_X))
                link(nc.vector.tensor_scalar(colc[:, 1], colc[:, 0], NEG / 10, None, ALU.max))
                nc.vector.tensor_tensor(lc[:], lc[:], colc[:, 1, :, None].to_broadcast([P, H, NC]), ALU.subtract)\
                    .then_inc(lc_ready, 1)
                dve.wait_ge(lc_exp, pair + 1)
                link(nc.vector.reduce_sum(colc[:, 2], lc[:], AX_X))
                link(nc.vector.tensor_scalar(colc[:, 2], colc[:, 2], 1e-30, None, ALU.max))
                link(nc.vector.reciprocal(colc[:, 3], colc[:, 2]))
                scaled = colc[:, 3].rearrange("p (t h) -> p t h", t=TT)
                link(nc.vector.tensor_tensor(scaled, scaled, gate[:, :, 0, heads], ALU.mult))
                nc.vector.tensor_tensor(pc[:, :, 0:NC], lc[:], colc[:, 3, :, None].to_broadcast([P, H, NC]), ALU.mult)\
                    .then_inc(pc_ready, 1)

            def attention(layer):
                chunk = START["out0"] if layer == 0 else START["kq1"]
                for n, beside in steps_of(layer):
                    if is_unit(layer, n - 5):
                        output_lo(n - 5)
                    if is_unit(layer, n):
                        largest(n)
                    split_to(chunk + AHEAD)
                    if is_unit(layer, n - 1):
                        scale(n - 1)
                    for what, *which in beside:
                        if what == "cmp_scores":
                            compressed(*which)
                        elif what == "cmp_turn":
                            pair = which[0]
                            dve.wait_ge(pcT_ready, pair + 1)
                            nc.vector.tensor_copy(pcT[:, 4 * pair:4 * pair + 4],
                                                  bank[2][:].rearrange("p (u q) -> p u q", q=P)).then_inc(pcT_copied, 1)
                        chunk += what in ("tile", "out") and which[-1]

            def ffn(layer):
                base = START[f"ffn{layer}"]

                def scale_gate_up(f, parity, done):
                    dve.wait_ge(chunk_done, done)
                    if not (layer == 0 and isinstance(f, int) and f < 2):
                        dve.wait_ge(hid_lo_ready, f + (layer * FT - 1))
                    nc.vector.tensor_tensor(silu[:, parity], bank[4 + parity][:, 0:S], rstd[:], ALU.mult)\
                        .then_inc(gate_scaled, 1)
                    nc.vector.tensor_tensor(hid[:, parity], bank[4 + parity][:, S:2 * S], rstd[:], ALU.mult)\
                        .then_inc(up_scaled, 1)

                def hidden(f, parity):
                    count = f + (layer * FT + 1)
                    dve.wait_ge(up_scaled, count)
                    dve.wait_ge(silu_ready, count)
                    nc.vector.tensor_tensor(hid[:, parity], hid[:, parity], silu[:, parity], ALU.mult)\
                        .then_inc(hid_ready, 1)

                def hidden_lo(f, parity):
                    dve.wait_ge(hid_hi_ready, f + (layer * FT + 1))
                    nc.vector.tensor_tensor(hid_lo[:, parity], hid[:, parity], f32(hid_hi[:, parity]), ALU.subtract)\
                        .then_inc(hid_lo_ready, 1)

                name, done = f"f{layer}", START[f"out{layer}"] + MIXT
                add_residual(done, 0)
                for b in range(4):
                    if b < 3:
                        add_residual(done, b + 1)
                    gained_lo(name, 2 * b)
                    gained_lo(name, 2 * b + 1)
                add_squares(name)
                split_to(base + 1 + AHEAD)
                inverse(name)
                for f in (0, 1):
                    scale_gate_up(f, f, base + 2 + 2 * f)
                    split_to(base + 2 + 2 * f + AHEAD)
                    hidden(f, f)
                    hidden_lo(f, f)
                if layer == 0:
                    for m in range(KT):
                        gained_lo("mem1", m)
                split_to(base + 5 + AHEAD)
                with dve.Fori(0, FFN_LOOPS) as i:
                    k = [0]
                    for j in (0, 1):
                        f = i * 2 + (2 + j)
                        split_loop(i, k, 1)
                        scale_gate_up(f, j, i * RING + (base + 5 + 3 * j + 2))
                        split_loop(i, k, 1)
                        hidden(f, j)
                        split_loop(i, k, 1)
                        hidden_lo(f, j)
                split[0] += FFN_LOOPS * RING
                for f in (FT - 2, FT - 1):
                    scale_gate_up(f, f % 2, base + 3 * f + 1)
                    split_to(base + 3 * f + 1 + AHEAD)
                    hidden(f, f % 2)
                    hidden_lo(f, f % 2)
                for b in range(4):
                    add_residual(LAST_DOWN[layer] + 1, b)
                add_squares("x1" if layer == 0 else "end")

            split_to(1)
            for m in range(KT):
                gained_lo("mem0", m)
            split_to(2)
            add_squares("mem0")
            split_to(3)
            add_squares("x0")
            inverse("mem0")
            split_to(4)
            inverse("x0")
            norm("x0")
            memory_keys(0, 0)
            memory_keys(0, 1)
            dve.wait_ge(table_ready, 1)
            nc.vector.tensor_copy(tab_row, bank[2][0:H, :]).then_inc(table_copied, 1)
            split_to(START["conv"] + AHEAD)
            per = 2 * 4
            conv_steps = steps[0]
            with dve.Fori(0, KT // 2) as i:
                k = [0]
                done = [0]

                def chain(ins):
                    done[0] += 1
                    ins.then_inc(dve_step, 1)
                    dve.wait_ge(dve_step, i * per + (conv_steps + done[0]))

                for j in (0, 1):
                    ft = i * 2 + j
                    split_loop(i, k, 2)
                    dve.wait_ge(c_copied, ft + 1)
                    chain(nc.vector.tensor_tensor(vpad[:, j, 2:S + 2], bank[j][:, S:2 * S], c_sb[:, j], ALU.mult))
                    chain(nc.vector.tensor_scalar(conv[:, j], vpad[:, j, 0:S], taps[:, 0, bass.ds(ft, 1)], None, ALU.mult))
                    for tap in (1, 2):
                        chain(nc.vector.scalar_tensor_tensor(out=conv[:, j], in0=vpad[:, j, tap:tap + S],
                                                             scalar=taps[:, tap, bass.ds(ft, 1)], in1=conv[:, j],
                                                             op0=ALU.mult, op1=ALU.add))
                    split_loop(i, k, 1)
                    dve.wait_ge(chunk_done, i * RING + (START["conv"] + 3 * j + 3))
                    nc.vector.tensor_tensor(conv[:, j], bank[4 + j][:, 0:S], conv[:, j], ALU.mult).then_inc(tok_ready, 1)
                    dve.wait_ge(tok_hi, ft + 1)
                    nc.vector.tensor_tensor(mix_lo[:, bass.ds(ft, 1)], conv[:, j:j + 1], f32(mix_hi[:, bass.ds(ft, 1)]),
                                            ALU.subtract).then_inc(tok_lo, 1)
                    dve.wait_ge(tok_lo, ft + 1)
                assert done[0] == per
            steps[0] += per * (KT // 2)
            split[0] += 3 * KT
            attention(0)
            split_to(START["ffn0"] + AHEAD)
            ffn(0)

            split_to(KEY_CHUNKS[1][2] + 1 + AHEAD)
            inverse("x1")
            norm("x1")
            memory_keys(1, 0)
            memory_keys(1, 1)
            split_to(START["cmp_k"] + AHEAD)

            def blocks(kv, part):
                for pair in range(2):
                    dve.wait_ge(chunk_done, START[part] + pair + 1)
                    for gg in range(2):
                        for half in range(2):
                            src = bank[2 + pair][64 * gg:64 * gg + 64, CS * half:CS * (half + NC)]
                            at = slice(64 * half, 64 * half + 64)
                            ins = nc.vector.tensor_tensor(
                                r_raw[at, :, 2 * pair + gg], src.rearrange("p (c l) -> p l c", l=CS),
                                pos[at, kv, :, None].to_broadcast([64, CS, NC]), ALU.add)
                ins.then_inc(blocks_ready, 1)

            def blocks_low(kv):
                dve.wait_ge(blocks_hi, kv + 1)
                nc.vector.tensor_tensor(r_lo[:], r_raw[:], f32(r_hi[:]), ALU.subtract).then_inc(blocks_lo, 1)

            split_to(START["cmp_k"] + 2 + AHEAD)
            blocks(0, "cmp_k")
            blocks_low(0)
            split_to(START["cmp_v"] + 2 + AHEAD)
            dve.wait_ge(blocks_lo, 1)
            blocks(1, "cmp_v")
            dve.wait_ge(kvc_ready, 1)
            nc.vector.tensor_copy(kc[:], bank[5][:, 0:G * NC].rearrange("p (g c) -> p g c", g=G))\
                .then_inc(kvc_copied, 1)
            dve.wait_ge(chunk_done, START["w1_k"] + 2)
            blocks_low(1)
            split_to(START["gates"] + AHEAD)
            dve.wait_ge(consts_set, CONSTS)
            dve.wait_ge(kvc_ready, 2)
            for a in range(HPG):
                nc.vector.tensor_copy(vc[32 * a:32 * a + NC, :, a * DK:(a + 1) * DK],
                                      bank[5][0:NC, 0:G * DK].rearrange("p (g d) -> p g d", g=G))\
                    .then_inc(kvc_copied, 1)
            split_to(START["gates"] + 1 + AHEAD)
            dve.wait_ge(gate_exp, 1)
            link(nc.vector.tensor_scalar(gate[:], gate[:], 1.0, None, ALU.add))
            link(nc.vector.reciprocal(gate[:], gate[:]))
            split_to(START["nat_v"] + COUNT["nat_v"] + AHEAD)
            dve.wait_ge(bias_loaded, 16)
            dve.wait_ge(consts_set, CONSTS)
            for t in range(TT):
                last = (t + 1) * P - CB
                blocks_seen = min(NC, last // CS + 1)
                stop = last - blocks_seen * CS
                ins = nc.vector.tensor_copy(bias_c[:, t, :, 0:blocks_seen],
                                            bias[:, :, last:(None if stop < 0 else stop):-CS])
            link(ins)
            attention(1)
            split_to(START["ffn1"] + AHEAD)
            ffn(1)
            inverse("end")
            for n in range(DVE_PAIRS):
                dve.wait_ge(out_gained, 2 * n + 2)
                out = mem[:, 2 * n:2 * n + 2]
                nc.vector.tensor_tensor(out, out, rstd[:, None].to_broadcast([P, 2, S]), ALU.mult).then_inc(out_ready, 1)

        @block.tensor
        def _(pe):
            def half_of(half):
                return range(KT) if half is None else range(half * KT // 2, (half + 1) * KT // 2)

            def three_passes(out, slot, cols, x_hi, x_lo, start, stop, **kw):
                nc.tensor.matmul(out, w_hi[:, slot, cols], x_hi, start=start, stop=False, **kw)
                nc.tensor.matmul(out, w_hi[:, slot, cols], x_lo, start=False, stop=False, **kw)
                return nc.tensor.matmul(out, w_lo[:, slot, cols], x_hi, start=False, stop=stop, **kw)

            def project(c, slot, out, x_hi, x_lo, normed=None, half=None):
                pe.wait_ge(lo_ready, c + 1)
                for kt in half_of(half):
                    if normed is not None:
                        pe.wait_ge(n_lo_ready, normed * KT + kt + 1)
                    ins = three_passes(out, slot, slice(kt * P, kt * P + P), x_hi[:, kt], x_lo[:, kt],
                                       kt == 0, kt == KT - 1)
                if half != 0:
                    ins.then_inc(chunk_done, 1)

            copied = [0]

            def project_tile(c, x_hi, x_lo, normed=None, half=None):
                if copied[0] >= 2:
                    pe.wait_ge(tile_copied, copied[0] - 1)
                project(c, c % RING, bank[copied[0] % 2][:, 0:S], x_hi, x_lo, normed, half)
                copied[0] += half != 0

            def project_tiles(part, x_hi, x_lo, normed=None):
                for n in range(COUNT[part]):
                    project_tile(START[part] + n, x_hi, x_lo, normed if n == 0 else None)

            def project_rows(part, x_hi, x_lo):
                if copied[0]:
                    pe.wait_ge(tile_copied, copied[0])
                for j in range(4):
                    c = START[part] + j
                    slot = c % RING
                    pe.wait_ge(lo_ready, c + 1)
                    for kt in (2 * j, 2 * j + 1):
                        cols = slice(kt % 2 * 512, kt % 2 * 512 + 512)
                        for t in range(TT):
                            at = slice(t * P, t * P + P)
                            nc.tensor.matmul(bank[t][:], x_hi[:, kt, at], w_hi[:, slot, cols], start=kt == 0, stop=False)
                            nc.tensor.matmul(bank[t][:], x_lo[:, kt, at], w_hi[:, slot, cols], start=False, stop=False)
                            ins = nc.tensor.matmul(bank[t][:], x_hi[:, kt, at], w_lo[:, slot, cols],
                                                   start=False, stop=kt == KT - 1)
                    ins.then_inc(chunk_done, 1)
                copied[0] += 2

            squares = [0]

            def sum_squares():
                k = squares[0]
                pe.wait_ge(sq_added, ADDS * (k + 1))
                if k:
                    pe.wait_ge(rms_ready, k)
                    pe.wait_ge(out_lo, outputs_before(FIRST_UNIT[(k - 1) // 2]))
                nc.tensor.matmul(bank[7][:, 0:S], ones[:], sq_sum[:, 0], start=True, stop=True).then_inc(sum_ready, 1)
                squares[0] += 1

            def accumulate(c, slot, x_hi, x_lo, first, last, half=None):
                pe.wait_ge(lo_ready, c + 1)
                for m in half_of(half):
                    ins = three_passes(bank[m // 2][:, m % 2 * S:m % 2 * S + S], slot, slice(m * P, m * P + P),
                                       x_hi, x_lo, first and m % 2 == 0, last, skip_group_check=True)
                    if last and m % 2 and m < KT - 1:
                        ins.then_inc(bank_done, 1)
                if half != 0:
                    ins.then_inc(chunk_done, 1)

            def query(g, a, t):
                return q_sb[64 * (g % 2):64 * (g % 2) + 64, 4 * (g // 2) + a, t * P:t * P + P]

            def scores(n):
                u, b = UNITS[n], bank[4 + n % 2]
                if n >= 2:
                    pe.wait_ge(exp_ready if UNITS[n - 2][0] == "mem" else max_ready, n - 1)
                if u[0] == "mem":
                    nc.tensor.matmul(b[:, 0:M], xq[:, u[1], u[2] * P:u[2] * P + P], mk[:, u[1]],
                                     start=True, stop=True).then_inc(scores_ready, 1)
                    return
                g, t, a = u[1:]
                for br in range(2):
                    ins = nc.tensor.matmul(b[:, br * S:br * S + (t + 1) * P], query(g, a, t),
                                           ks[64 * (g % 2):64 * (g % 2) + 64, br, g // 2, 0:(t + 1) * P],
                                           start=True, stop=True)
                ins.then_inc(scores_ready, 1)

            def turn(n):
                pe.wait_ge(prob_ready, n + 1)
                if n:
                    pe.wait_ge(probT_ready, n)
                blocks = keys_of(n)
                for at in range(blocks):
                    br, kt = (0, at) if UNITS[n][0] == "mem" else divmod(at, blocks // 2)
                    ins = nc.tensor.transpose(bank[6][:, at * P:at * P + P],
                                              att[:, n % 3, br, kt * P:kt * P + P], idt[:])
                ins.then_inc(turned, 1)

            def values(n):
                u = UNITS[n]
                if u[0] == "mem" and not makes_output(n):
                    return
                pe.wait_ge(probT_ready, n + 1)
                if outputs_before(n) and (u[0] == "mem" or u[3] == 0):
                    pe.wait_ge(out_lo, outputs_before(n))
                if u[0] == "mem":
                    for m in range(2):
                        ins = nc.tensor.matmul(bank[7][:, 0:S], mv[:, m, u[1] * P:u[1] * P + P], xprobT[:, m],
                                               start=m == 0, stop=m == 1)
                    ins.then_inc(values_done, 1)
                    return
                g, t, a = u[1:]
                if a == 0:
                    pe.wait_ge(pcT_copied, g // 2 + 1)
                    for half in range(2):
                        nc.tensor.matmul(bank[7][:, half * P:half * P + P], vc[:, g, half * P:half * P + P],
                                         pcT[:, g * TT + t], start=half == 0, stop=False, skip_group_check=True)
                for br in range(2):
                    for kt in range(t + 1):
                        last = a == HPG - 1 and br == 1 and kt == t
                        ins = nc.tensor.matmul(bank[7][DK * (a % 2):DK * (a % 2) + DK, a // 2 * P:a // 2 * P + P],
                                               v_nat[:, kt, br, g], probT[:, n % 2, br * (t + 1) + kt],
                                               start=False, stop=last, skip_group_check=True)
                ins.then_inc(values_done, 1)

            def compressed_scores(pair):
                pe.wait_ge(kvc_copied, 1 + HPG)
                if pair:
                    pe.wait_ge(pcT_copied, pair)
                for odd in range(2):
                    for t in range(TT):
                        for a in range(HPG):
                            at, g = t * HPG + a, 2 * pair + odd
                            ins = nc.tensor.matmul(cmp_bank(odd)[:, at * NC:(at + 1) * NC], query(g, a, t),
                                                   kc[64 * odd:64 * odd + 64, g], start=True, stop=True)
                ins.then_inc(sc_ready, 1)

            def compressed_turn(pair):
                pe.wait_ge(pc_ready, pair + 1)
                for k in range(2 * TT):
                    odd, t = divmod(k, TT)
                    at = (t * 2 + odd) * HPG
                    ins = nc.tensor.transpose(bank[2][:, k * P:k * P + P],
                                              pc[:, at:at + HPG].rearrange("p h c -> p (h c)"), idt[:])
                ins.then_inc(pcT_ready, 1)

            def mix_out(layer, j, half=None):
                c, kt = START[f"out{layer}"] + j, OUT_ORDER[layer][j]
                if j == 0:
                    pe.wait_ge(tile_copied, copied[0])
                    pe.wait_ge(pcT_copied, 2) if layer else pe.wait_ge(tok_lo, KT)
                if layer or kt >= KT:
                    unit = [n for n in range(FIRST_UNIT[layer], FIRST_UNIT[layer + 1]) if makes_output(n)
                            and (UNITS[n][:2] == ("mem", kt - KT) if kt >= KT
                                 else UNITS[n][0] == "nsa" and UNITS[n][1] == kt // 2)][-1]
                    pe.wait_ge(out_lo, outputs_before(unit) + 1)
                accumulate(c, c % RING, mix_hi[:, kt], mix_lo[:, kt], j == 0, j == MIXT - 1, half)

            def attention(layer):
                chunk, outs = (START["out0"] if layer == 0 else START["kq1"]), 0
                for n, beside in steps_of(layer):
                    if is_unit(layer, n - 3):
                        turn(n - 3)
                    if is_unit(layer, n):
                        scores(n)
                    if is_unit(layer, n - 4) and UNITS[n - 4][-1] > 0:
                        values(n - 4)
                    for what, *which in beside:
                        if what == "tile":
                            project_tile(chunk, n_hi, n_lo, half=which[-1])
                        elif what == "out":
                            mix_out(layer, *which)
                            outs += which[-1]
                        elif what == "cmp_scores":
                            compressed_scores(*which)
                        else:
                            compressed_turn(*which)
                        chunk += what in ("tile", "out") and which[-1]
                    if is_unit(layer, n - 4) and UNITS[n - 4][-1] == 0:
                        values(n - 4)
                for j in range(outs, MIXT):
                    mix_out(layer, j)

            def ffn(layer):
                base = START[f"ffn{layer}"]

                def gate_up(f, parity, c, slot, normed=None):
                    if not (layer == 0 and isinstance(f, int) and f < 2):
                        pe.wait_ge(up_scaled, f + (layer * FT - 1))
                    for j in range(2):
                        project(c + j, (slot + j) % RING, bank[4 + parity][:, j * S:j * S + S], n_hi, n_lo,
                                normed if j == 0 else None)

                def down(f, parity, c, slot, first=False, last=False):
                    pe.wait_ge(hid_lo_ready, f + (layer * FT + 1))
                    accumulate(c, slot % RING, hid_hi[:, parity], hid_lo[:, parity], first, last)

                gate_up(0, 0, base, base, NORMS.index(f"f{layer}"))
                sum_squares()
                gate_up(1, 1, base + 2, base + 2)
                down(0, 0, base + 4, base + 4, first=True)
                with pe.Fori(0, FFN_LOOPS) as i:
                    for j in (0, 1):
                        c = base + 5 + 3 * j
                        gate_up(i * 2 + (2 + j), j, i * RING + c, c)
                        down(i * 2 + (1 + j), 1 - j, i * RING + (c + 2), c + 2)
                for f in (FT - 2, FT - 1):
                    c = base + 3 * f - 1
                    gate_up(f, f % 2, c, c)
                    down(f - 1, (f - 1) % 2, c + 2, c + 2)
                if layer == 0:
                    pe.wait_ge(up_scaled, FT - 1)
                    memory_key(1, 0)
                    memory_key(1, 1)
                down(FT - 1, (FT - 1) % 2, LAST_DOWN[layer], LAST_DOWN[layer], last=True)
                if layer == 0:
                    pe.wait_ge(up_scaled, FT)

            def memory_key(layer, a, normed=None):
                c = KEY_CHUNKS[layer][a]
                project(c, c % RING, bank[4 + a // 2][:, a % 2 * M:a % 2 * M + M], m_hi, m_lo, normed)

            memory_key(0, 0, NORMS.index("mem0"))
            memory_key(0, 1)
            pe.wait_ge(consts_set, CONSTS)
            sum_squares()
            memory_key(0, 2)
            sum_squares()
            memory_key(0, 3)
            pe.wait_ge(small_loaded, SMALL)
            nc.tensor.matmul(bank[2][0:H, :], tab[:], fwd, start=True, stop=True).then_inc(table_ready, 1)
            project_rows("mem_v0", m_hi, m_lo)
            pe.wait_ge(rstd_ready, 1)
            for t in range(TT):
                ins = nc.tensor.matmul(bank[6][:, t:t + 1], mem_rstd[:, t * P:t * P + P], idt[:, 0:1],
                                       start=True, stop=True)
            ins.then_inc(rcol_ready, 1)
            pe.wait_ge(n_lo_ready, 2 * KT)
            project_tiles("xq0", n_hi, n_lo)

            def conv_tile(j, c, slot):
                project(c, slot % RING, bank[j][:, 0:S], n_hi, n_lo)
                project(c + 1, (slot + 1) % RING, bank[j][:, S:2 * S], n_hi, n_lo)
                project(c + 2, (slot + 2) % RING, bank[4 + j][:, 0:S], n_hi, n_lo)

            pe.wait_ge(tile_copied, copied[0])
            pe.wait_ge(mk_copied, 2)
            base = START["conv"]
            for j in (0, 1):
                conv_tile(j, base + 3 * j, base + 3 * j)
            with pe.Fori(1, KT // 2) as i:
                for j in (0, 1):
                    pe.wait_ge(tok_ready, i * 2 + (j - 1))
                    conv_tile(j, i * RING + (base + 3 * j), base + 3 * j)
            pe.wait_ge(tok_ready, KT)
            pe.wait_ge(table_copied, 1)
            attention(0)
            ffn(0)

            memory_key(1, 2)
            sum_squares()
            memory_key(1, 3)
            pe.wait_ge(residual_added, KT)
            project_rows("mem_v1", m_hi, m_lo)

            def raw_blocks(part, normed=None):
                for pair in range(2):
                    c = START[part] + pair
                    project(c, c % RING, bank[2 + pair][:, 0:S], n_hi, n_lo, None if pair else normed)

            def hidden(kv, part):
                pe.wait_ge(blocks_lo, kv + 1)
                for j in range(2):
                    c = START[part] + j
                    pe.wait_ge(lo_ready, c + 1)
                    for l in range(8):
                        ll = 8 * j + l
                        ins = three_passes(bank[4][:, 0:G * NC], c % RING, slice(l * P, l * P + P),
                                           r_hi[:, ll].rearrange("p g c -> p (g c)"),
                                           r_lo[:, ll].rearrange("p g c -> p (g c)"), ll == 0, ll == CS - 1)
                    ins.then_inc(chunk_done, 1)

            raw_blocks("cmp_k", NORMS.index("x1"))
            project_tiles("kq0", n_hi, n_lo)
            pe.wait_ge(mk_copied, 4)
            hidden(0, "w1_k")
            pe.wait_ge(blocks_ready, 1)
            raw_blocks("cmp_v")
            pe.wait_ge(hmid_ready, 1)
            nc.tensor.matmul(bank[5][:, 0:G * NC], w2[:, 0], hmid[:, 0], start=True, stop=True).then_inc(kvc_ready, 1)
            project_tiles("q0", n_hi, n_lo)
            hidden(1, "w1_v")
            c = START["gates"]
            pe.wait_ge(lo_ready, c + 1)
            for t in range(TT):
                at, out = slice(t * P, t * P + P), bank[6][:, t * 3 * H:(t + 1) * 3 * H]
                for kt in range(KT):
                    cols = slice(kt * 3 * H, (kt + 1) * 3 * H)
                    nc.tensor.matmul(out, n_hi[:, kt, at], w_hi[:, c % RING, cols], start=kt == 0, stop=False)
                    nc.tensor.matmul(out, n_lo[:, kt, at], w_hi[:, c % RING, cols], start=False, stop=False)
                    ins = nc.tensor.matmul(out, n_hi[:, kt, at], w_lo[:, c % RING, cols], start=False, stop=kt == KT - 1)
            ins.then_inc(chunk_done, 1)
            pe.wait_ge(hmid_ready, 2)
            pe.wait_ge(kvc_copied, 1)
            for g in range(G):
                ins = nc.tensor.matmul(bank[5][0:NC, g * DK:(g + 1) * DK], hmid[:, 1, g * NC:(g + 1) * NC],
                                       w2[:, 1, 0:DK], start=True, stop=True)
            ins.then_inc(kvc_ready, 1)
            project_rows("nat_v", n_hi, n_lo)
            pe.wait_ge(tile_copied, copied[0])
            pe.wait_ge(gate_exp, 1)
            pe.wait_ge(blocks_ready, 2)
            attention(1)
            ffn(1)
            sum_squares()


def layout(x):
    def tiles(w):
        k, n = w.shape
        return w.reshape(k // P, P, n // P, P).transpose(2, 1, 0, 3).reshape(n // P, P, k)

    def rows(w):
        return w.reshape(4, 2, P, 512).transpose(0, 2, 1, 3).reshape(4, P, CHUNK)

    def by_input(w):
        return w.reshape(-1, P, CHUNK)

    conv, nsa = x["w_in_conv"][0], x["w_in_nsa"][0]
    kv0 = H * DK
    kvs = [nsa[:, kv0 + i * G * DK:kv0 + (i + 1) * G * DK] for i in range(6)]
    gates = nsa[:, kv0 + 6 * G * DK:kv0 + 6 * G * DK + 3 * H]
    q = nsa[:, :H * DK].reshape(D, G // 2, 2, HPG, DK).transpose(0, 1, 3, 2, 4).reshape(D, H * DK)
    gate_chunk = np.zeros((1, P, CHUNK), np.float32)
    gate_chunk[0, :, :KT * 3 * H] = gates.reshape(KT, P, 3 * H).transpose(1, 0, 2).reshape(P, KT * 3 * H)

    def w1(w):
        w = w.reshape(2, CS, DK, P).transpose(0, 2, 1, 3).reshape(P, 2, CHUNK)
        return w.transpose(1, 0, 2)

    def ffn(i):
        w = tiles(x["w_ffn_in"][i])
        gate, up, out = w[:FT], w[FT:], by_input(x["w_ffn_out"][i])
        parts = [gate[0], up[0]]
        for f in range(1, FT):
            parts += [gate[f], up[f], out[f - 1]]
        return np.stack(parts + [out[FT - 1]])

    b, c, u = (tiles(conv[:, i * D:(i + 1) * D]) for i in range(3))
    parts = {
        "conv": np.stack([c, u, b], 1).reshape(3 * KT, P, CHUNK),
        "xq0": tiles(conv[:, 3 * D:]), "xq1": tiles(nsa[:, -XH * P:]),
        "cmp_k": tiles(kvs[0]), "cmp_v": tiles(kvs[1]),
        "w1_k": w1(x["cmp_w1_k"][0]), "w1_v": w1(x["cmp_w1_v"][0]),
        "nat_v": rows(np.concatenate([kvs[3], kvs[5]], 1)), "gates": gate_chunk,
    }
    for i in range(2):
        parts[f"kq{i}"] = np.concatenate([tiles(kvs[2])[i:i + 1], tiles(kvs[4])[i:i + 1], tiles(q)[4 * i:4 * i + 4]])
        parts[f"mem_k{i}"] = tiles(x["w_mem_kv"][i][:, :XH * P])
        parts[f"mem_v{i}"] = rows(x["w_mem_kv"][i][:, XH * P:])
        parts[f"out{i}"] = by_input(x["w_out"][i])[OUT_ORDER[i]]
        parts[f"ffn{i}"] = ffn(i)
    parts["kq0"], parts["q0"] = parts["kq0"][:3], parts["kq0"][3:]
    parts["mem_k1"] = np.concatenate([parts["mem_k1"][:2], parts["ffn0"][-1:], parts["mem_k1"][2:]])
    parts["ffn0"] = parts["ffn0"][:-1]
    for name, count in PARTS:
        assert parts[name].shape == (count, P, CHUNK), name

    def features(a):
        return a.reshape(-1, KT, P).transpose(2, 1, 0)

    gains = np.stack([x["norm_mem_g"][0], x["norm_mix_g"][0], x["norm_ffn_g"][0],
                      x["norm_mem_g"][1], x["norm_mix_g"][1], x["norm_ffn_g"][1], x["norm_final_g"]])

    def positions(p):
        return p.reshape(2, CS, DK).transpose(0, 2, 1).reshape(P, CS)

    dist = np.arange(-DIST0, DIST0)
    near = BUCKETS // 2
    far = near + (np.log(np.maximum(dist, 1).astype(np.float32) / np.float32(near))
                  / np.float32(np.log(128 / near)) * (BUCKETS - near)).astype(np.int32)
    bucket = np.where(dist < 0, BUCKETS, np.where(dist < near, dist, np.minimum(far, BUCKETS - 1)))
    forward = (np.arange(BUCKETS + 1)[:, None] == bucket).astype(np.float32)
    return {
        "stream": np.concatenate([parts[name] for name, _ in PARTS]),
        "xT": features(x["x"][0]), "memT": features(x["mem"][0]),
        "gains": features(gains).transpose(0, 2, 1),
        "conv_w": features(x["conv_w"][0]).transpose(0, 2, 1),
        "cmp_pos": np.stack([positions(x["cmp_pos_k"][0]), positions(x["cmp_pos_v"][0])], 1),
        "cmp_w2": np.stack([np.concatenate([w[0], w[0]], 1) for w in (x["cmp_w2_k"], x["cmp_w2_v"])], 1),
        "rel_bias": x["rel_bias"], "dist_fwd": forward,
        "ident": np.eye(P, dtype=np.float32),
    }


def kernel(**inputs):
    import concourse.bacc as bacc
    from concourse.bass_utils import run_bass_kernel_spmd

    arrays = layout({k: np.asarray(v) for k, v in inputs.items()})
    arrays = {k: np.ascontiguousarray(v) for k, v in arrays.items()}
    nc = bacc.Bacc("TRN2", target_bir_lowering=False, num_devices=1)
    args = {k: nc.dram_tensor(k, a.shape, mybir.dt.from_np(a.dtype), kind="ExternalInput").ap()
            for k, a in arrays.items()}
    outT = nc.dram_tensor("outT", (P, KT, S), F32, kind="ExternalOutput").ap()
    build(nc, outT=outT, **args)
    got = run_bass_kernel_spmd(nc, [arrays], core_ids=[0]).results[0]["outT"]
    return np.ascontiguousarray(np.asarray(got).transpose(2, 1, 0).reshape(1, S, D))
```

```python
from contextlib import ExitStack

import numpy as np

import concourse.bass as bass
from concourse import mybir

ALU = mybir.AluOpType
ACT = mybir.ActivationFunctionType
AX_X = mybir.AxisListType.X
F32 = mybir.dt.float32
F32R = mybir.dt.float32r

P = 128
D, S, M = 1024, 256, 256
KT = D // P
TT = S // P
XH = 4
H, G, HPG, DK = 16, 4, 4, 64
MIXT = (D + XH * P) // P
FT = 2816 // P
CB, CS = 32, 16
NC = (S - CB) // CS + 1
BUCKETS = 32
CHUNK = 8 * P
RING = 6
RAW = RING // 2
AHEAD = 5
EPS = 1e-6
NEG = -1e30
FFN_LOOPS = (FT - 4) // 2
CONSTS = 7
SMALL = 16 * 6
XSCALE = float(P) ** -0.5
SCALE = float(DK) ** -0.5
DIST0 = S

PARTS = [("mem_k0", 4), ("mem_v0", 4), ("conv", 3 * KT), ("xq0", 4), ("out0", MIXT), ("ffn0", 3 * FT - 1),
         ("mem_k1", 5), ("mem_v1", 4), ("cmp_k", 2), ("kq0", 3), ("w1_k", 2), ("cmp_v", 2), ("q0", 3), ("w1_v", 2),
         ("gates", 1), ("nat_v", 4), ("kq1", 6), ("xq1", 4), ("out1", MIXT), ("ffn1", 3 * FT)]
START, TOTAL = {}, 0
for _name, _count in PARTS:
    START[_name] = TOTAL
    TOTAL += _count
COUNT = dict(PARTS)
LAST_DOWN = [START["mem_k1"] + 2, START["ffn1"] + 3 * FT - 1]
KEY_CHUNKS = [[START["mem_k0"] + a for a in range(XH)], [START["mem_k1"] + a for a in (0, 1, 3, 4)]]

MEM_UNITS = [("mem", a, t) for a in range(XH) for t in range(TT)]
NSA_UNITS = [[("nsa", g, t, a) for t in range(TT) for a in range(HPG)] for g in range(G)]
UNITS = MEM_UNITS + NSA_UNITS[0] + NSA_UNITS[1] + MEM_UNITS + NSA_UNITS[2] + NSA_UNITS[3]
FIRST_UNIT = [0, len(MEM_UNITS), len(UNITS)]
DRAIN = 5

OUT_ORDER = [list(range(MIXT)), [0, 1, 2, 3, 8, 9, 10, 11, 4, 5, 6, 7]]


def halves(items, starts):
    return [(r + half, item + (half,)) for item, r in zip(items, starts) for half in range(2)]


def by_step(pairs):
    return {r: [item for at, item in pairs if at == r] for r, _ in pairs}


BESIDE = [
    by_step([(r, ("out", j, half)) for j, r in enumerate([*range(KT), 9, 11, 12]) for half in range(2)]),
    by_step([(1, ("cmp_scores", 0)), (3, ("cmp_turn", 0)), (13, ("cmp_scores", 1)), (15, ("cmp_turn", 1))]
            + halves([("tile", "kq1", j) for j in range(6)], range(0, 12, 2))
            + halves([("tile", "xq1", j) for j in range(XH)], range(12, 20, 2))
            + halves([("out", j) for j in range(10)], [*range(20, 36, 2), 37, 39])),
]


def steps_of(layer):
    first, end = FIRST_UNIT[layer], FIRST_UNIT[layer + 1]
    return [(n, BESIDE[layer].get(n - first, [])) for n in range(first, end + DRAIN)]


def is_unit(layer, n):
    return FIRST_UNIT[layer] <= n < FIRST_UNIT[layer + 1]


def makes_output(n):
    return UNITS[n][2] == TT - 1 if UNITS[n][0] == "mem" else UNITS[n][3] == HPG - 1


def outputs_before(n, kind=None):
    return sum(makes_output(m) and kind in (None, UNITS[m][0]) for m in range(n))


def values_through(n):
    return sum(UNITS[m][0] == "nsa" or makes_output(m) for m in range(n + 1))


def keys_of(n):
    return TT if UNITS[n][0] == "mem" else 2 * (UNITS[n][2] + 1)


def build(nc, stream, xT, memT, gains, conv_w, cmp_pos, cmp_w2, rel_bias, dist_fwd, ident, outT):
    table_dram = nc.dram_tensor("bias_by_distance", (H, 2 * S), F32, kind="Internal").ap()
    with ExitStack() as ctx:
        def sb(name, shape, dt=F32):
            return ctx.enter_context(nc.sbuf_tensor(name, shape, dt))

        def sem(name):
            return ctx.enter_context(nc.semaphore(name))

        raw = sb("raw", [P, RAW, CHUNK])
        w_hi = sb("w_hi", [P, RING, CHUNK], F32R)
        w_lo = sb("w_lo", [P, RING, CHUNK], F32R)
        h = sb("h", [P, KT, S])
        mem = sb("mem", [P, KT, M])
        n_hi = sb("n_hi", [P, KT, S], F32R)
        n_lo = sb("n_lo", [P, KT, S], F32R)
        mix_hi = sb("mix_hi", [P, MIXT, S], F32R)
        mix_lo = sb("mix_lo", [P, MIXT, S], F32R)
        m_hi, m_lo = mix_hi[:, 0:KT], mix_lo[:, 0:KT]
        sq_sum = sb("sq_sum", [P, 2, S])
        rms = sb("rms", [P, S])
        rstd = sb("rstd", [P, S])
        mem_rstd = sb("mem_rstd", [P, M])
        rstd_sq = sb("rstd_sq", [P, S])
        rcol = sb("rcol", [P, 3, TT])
        gain = sb("gain", [P, 7, KT])
        taps = sb("taps", [P, 3, KT])
        ones = sb("ones", [P, P])
        idt = sb("idt", [P, P])
        eps = sb("eps", [P, 1])
        warm = sb("warm", [P, 1])
        tab = sb("tab", [BUCKETS + 1, H])
        bias = sb("bias", [P, H, S])
        bias_c = sb("bias_c", [P, TT, H, NC])
        pos = sb("pos", [P, 2, CS])
        w2 = sb("w2", [P, 2, P])
        xq = sb("xq", [P, XH, S])
        mk = sb("mk", [P, XH, M])
        mv = sb("mv", [P, 2, XH * P])
        silu = sb("silu", [P, 2, S])
        hid = sb("hid", [P, 2, S])
        hid_hi = sb("hid_hi", [P, 2, S], F32R)
        hid_lo = sb("hid_lo", [P, 2, S], F32R)
        q_sb = mem
        ks = sb("ks", [P, 2, 2, S])
        v_nat = sb("v_nat", [P, TT, 2, G, DK])
        gate = sb("gate", [P, TT, 3, H])
        c_sb = v_nat[:, 0].rearrange("p b g d -> p b (g d)")
        conv = v_nat[:, 1].rearrange("p b g d -> p b (g d)")
        vpad = ks[:].rearrange("p b a s -> p (b a s)")[:, 0:2 * (S + 2)].rearrange("p (b s) -> p b s", b=2)
        r_split = sb("r_split", [P, CS, 2, G * NC], F32R)
        hmid = sb("hmid", [P, 2, G * NC])
        kc = sb("kc", [P, G, NC])
        vc = sb("vc", [P, G, HPG * DK])
        lc = sb("lc", [P, H, NC])
        pc = sb("pc", [P, H, 32])
        pcT = sb("pcT", [P, G * TT, P])
        att = sb("att", [P, 3, 2, S])
        probT = sb("probT", [P, 2, 4, P])
        xprobT = sb("xprobT", [P, 2, TT, P])
        fwd = att[0:BUCKETS + 1, 1].rearrange("p b s -> p (b s)")
        tab_row = att[0:H, 2].rearrange("p b s -> p (b s)")
        r_raw = att[:].rearrange("p a b s -> p (a b s)")[:, 0:CS * G * NC]\
            .rearrange("p (l x) -> p l x", l=CS)
        sq = {name: [silu, hid] * 2 for name in ("mem0", "x0", "f0", "x1", "f1")}
        sq["end"] = [silu, hid, att[:, 0], att[:, 1]]
        col = sb("col", [P, 3, 4, 2])
        colc = sb("colc", [P, 4, H])

        bank = [ctx.enter_context(nc.psum_tensor(f"bank{i}", [P, 512], F32)) for i in range(8)]

        raw_loaded = [sem(f"raw_loaded{i}") for i in range(RAW)]
        hi_ready = sem("hi_ready")
        lo_ready = sem("lo_ready")
        chunk_done = sem("chunk_done")
        gain_loaded = sem("gain_loaded")
        x_loaded = sem("x_loaded")
        mem_loaded = [sem(f"mem_loaded{i}") for i in range(2)]
        small_loaded = sem("small_loaded")
        consts_set = sem("consts_set")
        table_ready = sem("table_ready")
        table_copied = sem("table_copied")
        table_stored = sem("table_stored")
        bias_loaded = sem("bias_loaded")
        dve_step = sem("dve_step")
        out_gained = sem("out_gained")
        out_ready = sem("out_ready")
        pool_out_ready = sem("pool_out_ready")
        out_stored = sem("out_stored")

        NORMS = ["mem0", "x0", "f0", "mem1", "x1", "f1", "end"]
        sq_ready = sem("sq_ready")
        sq_added = sem("sq_added")
        sum_ready = sem("sum_ready")
        rms_ready = sem("rms_ready")
        rstd_ready = sem("rstd_ready")
        n_hi_ready = sem("n_hi_ready")
        n_lo_ready = sem("n_lo_ready")
        bank_done = sem("bank_done")
        residual_added = sem("residual_added")
        rcol_ready = sem("rcol_ready")
        rcol_copied = sem("rcol_copied")
        mk_copied = sem("mk_copied")

        tile_copied = sem("tile_copied")
        rows_copied = sem("rows_copied")
        c_copied = sem("c_copied")
        tok_ready = sem("tok_ready")
        tok_hi = sem("tok_hi")
        tok_lo = sem("tok_lo")
        gate_scaled = sem("gate_scaled")
        up_scaled = sem("up_scaled")
        silu_ready = sem("silu_ready")
        hid_ready = sem("hid_ready")
        hid_hi_ready = sem("hid_hi_ready")
        hid_lo_ready = sem("hid_lo_ready")
        blocks_ready = sem("blocks_ready")
        blocks_hi = sem("blocks_hi")
        blocks_lo = sem("blocks_lo")
        hmid_copied = sem("hmid_copied")
        hmid_summed = sem("hmid_summed")
        hmid_ready = sem("hmid_ready")
        kvc_ready = sem("kvc_ready")
        kvc_copied = sem("kvc_copied")
        gate_exp = sem("gate_exp")
        sc_ready = sem("sc_ready")
        lc_ready = sem("lc_ready")
        lc_exp = sem("lc_exp")
        pc_ready = sem("pc_ready")
        pcT_ready = sem("pcT_ready")
        pcT_copied = sem("pcT_copied")
        scores_ready = sem("scores_ready")
        max_ready = sem("max_ready")
        exp_ready = sem("exp_ready")
        prob_ready = sem("prob_ready")
        turned = sem("turned")
        probT_ready = sem("probT_ready")
        values_done = sem("values_done")
        out_hi = sem("out_hi")
        out_lo = sem("out_lo")

        def f32(ap):
            return ap.bitcast(F32)

        SUMMED = ["mem0", "x0", "f0", "x1", "f1", "end"]
        DVE_PAIRS = 3
        ADDS = KT // 2

        def norm_source(name):
            return mem if name.startswith("mem") else h

        def cmp_bank(odd):
            return bank[2 + odd]

        def tile_target(part, j):
            if part.startswith("xq"):
                return xq[:, j], XSCALE
            if part == "q0":
                return q_sb[:, 1 + j], SCALE
            pair = int(part[-1])
            return (ks[:, j, pair], 1.0) if j < 2 else (q_sb[:, 4 * pair + j - 2], SCALE)

        def output_of(n, mix):
            u = UNITS[n]
            return mix[:, KT + u[1]] if u[0] == "mem" else mix[:, 2 * u[1]:2 * u[1] + 2, u[2] * P:u[2] * P + P]

        def output_psum(n):
            return bank[7][:, 0:S] if UNITS[n][0] == "mem" else bank[7][:, 0:S].rearrange("p (h q) -> p h q", h=2)

        block = ctx.enter_context(nc.Block())

        @block.sync
        def _(sp):
            def load(c, slot):
                sp.dma_start(raw[:, slot], stream[c]).then_inc(raw_loaded[slot], 16)

            load(0, 0)
            sp.dma_start(gain[:], gains).then_inc(gain_loaded, 16)
            for i in range(2):
                half = slice(i * KT // 2, (i + 1) * KT // 2)
                sp.dma_start(mem[:, half], memT[:, half]).then_inc(mem_loaded[i], 16)
            load(1, 1)
            sp.dma_start(h[:], xT).then_inc(x_loaded, 16)
            load(2, 2)
            full = TOTAL // RAW
            with sp.Fori(1, full) as i:
                for slot in range(RAW):
                    sp.wait_ge(lo_ready, i * RAW + (slot + 1 - RAW))
                    load(i * RAW + slot, slot)
            for c in range(full * RAW, TOTAL):
                sp.wait_ge(lo_ready, c - RAW + 1)
                load(c, c % RAW)
            for n in range(DVE_PAIRS):
                sp.wait_ge(out_ready, n + 1)
                sp.dma_start(outT[:, 2 * n:2 * n + 2], mem[:, 2 * n:2 * n + 2]).then_inc(out_stored, 16)
            sp.wait_ge(pool_out_ready, 1)
            sp.dma_start(outT[:, 2 * DVE_PAIRS:KT], mem[:, 2 * DVE_PAIRS:KT]).then_inc(out_stored, 16)
            sp.wait_ge(out_stored, 16 * (DVE_PAIRS + 1))

        @block.gpsimd
        def _(pool):
            for n, (tile, value) in enumerate(((ones, 1.0), (eps, EPS), (vpad, 0.0),
                                               (bias_c, NEG), (tab[BUCKETS:BUCKETS + 1, :], NEG), (pc, 0.0),
                                               (vc, 0.0))):
                if n:
                    pool.wait_ge(consts_set, n)
                nc.gpsimd.memset(tile if tile.shape[0] == 1 else tile[:], value).then_inc(consts_set, 1)
                if n == 1:
                    for small, src in ((tab[0:BUCKETS, :], rel_bias), (fwd, dist_fwd), (idt[:], ident),
                                       (taps[:], conv_w), (pos[:], cmp_pos), (w2[:], cmp_w2)):
                        pool.dma_start(small, src).then_inc(small_loaded, 16)
            pool.wait_ge(table_copied, 1)
            pool.dma_start(table_dram, tab_row).then_inc(table_stored, 16)
            pool.wait_ge(table_stored, 16)
            pool.wait_ge(chunk_done, START["conv"])
            rows = bass.AP(tensor=table_dram.tensor, offset=DIST0 - (P - 1), ap=[[1, P], [2 * S, H], [1, S]])
            pool.dma_start(bias[:], rows).then_inc(bias_loaded, 16)
            pool.wait_ge(bias_loaded, 16)
            pool.wait_ge(out_gained, KT)
            pool.wait_ge(rstd_ready, len(SUMMED))
            rest = mem[:, 2 * DVE_PAIRS:KT]
            nc.gpsimd.tensor_tensor(rest, rest, rstd[:, None].to_broadcast([P, KT - 2 * DVE_PAIRS, S]), ALU.mult)\
                .then_inc(pool_out_ready, 1)

        @block.scalar
        def _(act):
            split = [0]

            def split_hi(c, slot, landed, may_wait=True):
                act.wait_ge(raw_loaded[slot % RAW], landed)
                if may_wait:
                    act.wait_ge(chunk_done, c - RING + 1)
                nc.scalar.copy(w_hi[:, slot], raw[:, slot % RAW]).then_inc(hi_ready, 1)

            def split_to(end):
                while split[0] < min(end, TOTAL):
                    c = split[0]
                    split_hi(c, c % RING, 16 * (c // RAW + 1), c >= RING)
                    split[0] += 1

            def split_loop(i, k, count):
                for _ in range(count):
                    c = split[0] + k[0]
                    split_hi(i * RING + c, c % RING, i * (16 * RING // RAW) + 16 * (c // RAW + 1))
                    k[0] += 1

            def copy_rows(part, outs, banks, factor):
                split_to(START[part] + 4 + AHEAD)
                act.wait_ge(chunk_done, START[part] + 4)
                for t, out in enumerate(outs):
                    nc.scalar.mul(out, bank[banks[t]][:], rcol[:, factor, t:t + 1]).then_inc(rows_copied, 1)

            def columns(k, factor):
                act.wait_ge(rcol_ready, k)
                nc.scalar.copy(rcol[:, factor], bank[7][:, 0:TT]).then_inc(rcol_copied, 1)

            def gained(name):
                src, hi = (mem, m_hi) if name.startswith("mem") else (h, n_hi)
                act.wait_ge(gain_loaded, 16)
                for m in range(KT):
                    if name == "mem0":
                        act.wait_ge(mem_loaded[m // (KT // 2)], 16)
                    elif name == "x0":
                        act.wait_ge(x_loaded, 16)
                    elif name != "mem1":
                        act.wait_ge(residual_added, KT // 2 * (SUMMED.index(name) - 2) + m // 2 + 1)
                    nc.scalar.mul(hi[:, m], src[:, m], gain[:, NORMS.index(name), m:m + 1]).then_inc(n_hi_ready, 1)

            def square(name):
                src, k = norm_source(name), SUMMED.index(name)
                for m in range(KT // 2):
                    if name == "mem0":
                        act.wait_ge(mem_loaded[1], 16)
                    elif name == "x0":
                        act.wait_ge(x_loaded, 16)
                    else:
                        act.wait_ge(residual_added, KT // 2 * (k - 2) + m + 1)
                    if m >= 2 and name != "end":
                        act.wait_ge(sq_added, ADDS * k + 1)
                    elif k:
                        act.wait_ge(sq_added, ADDS * k)
                    nc.scalar.activation(sq[name][m][:], src[:, 2 * m:2 * m + 2], ACT.Square).then_inc(sq_ready, 1)

            def root(name):
                k = SUMMED.index(name)
                act.wait_ge(sum_ready, k + 1)
                if k:
                    act.wait_ge(rstd_ready, k)
                act.wait_ge(consts_set, CONSTS)
                nc.scalar.activation(rms[:], bank[7][:, 0:S], ACT.Sqrt, bias=eps[:, 0:1],
                                     scale=1.0 / D).then_inc(rms_ready, 1)

            def exp(n):
                u, k, b = UNITS[n], n % 3, bank[4 + n % 2]
                act.wait_ge(max_ready, n + 1)
                if u[0] == "mem":
                    nc.scalar.activation(att[:, k, 0], b[:, 0:M], ACT.Exp, bias=col[:, k, 0, 0:1],
                                         accum_out=col[:, k, 1, 0:1]).then_inc(exp_ready, 1)
                    return
                keys = (u[2] + 1) * P
                for br in range(2):
                    ins = nc.scalar.activation(att[:, k, br, 0:keys], att[:, k, br, 0:keys], ACT.Exp,
                                               bias=col[:, k, 0, br:br + 1], accum_out=col[:, k, 1, br:br + 1])
                ins.then_inc(exp_ready, 1)

            def copy_turned(n):
                u = UNITS[n]
                act.wait_ge(turned, n + 1)
                if u[0] == "mem":
                    if u[2] == 0 and outputs_before(n, "mem"):
                        last = max(m for m in range(n) if UNITS[m][0] == "mem")
                        act.wait_ge(values_done, values_through(last))
                    out, blocks = xprobT[:, :, u[2]], TT
                else:
                    before = [m for m in range(n) if UNITS[m][0] == "nsa" and m % 2 == n % 2]
                    if before:
                        act.wait_ge(values_done, values_through(before[-1]))
                    blocks = keys_of(n)
                    out = probT[:, n % 2, 0:blocks]
                nc.scalar.copy(out, bank[6][:, 0:blocks * P].rearrange("p (b q) -> p b q", q=P)).then_inc(probT_ready, 1)

            def output_hi(n):
                if not makes_output(n):
                    return
                u = UNITS[n]
                act.wait_ge(values_done, values_through(n))
                nc.scalar.copy(output_of(n, mix_hi), output_psum(n)).then_inc(out_hi, 1)

            def attention(layer):
                chunk = START["out0"] if layer == 0 else START["kq1"]
                for n, beside in steps_of(layer):
                    split_to(chunk + AHEAD)
                    if is_unit(layer, n - 3):
                        copy_turned(n - 3)
                    if is_unit(layer, n):
                        exp(n)
                    if is_unit(layer, n - 4):
                        output_hi(n - 4)
                    for what, *which in beside:
                        if what == "cmp_scores":
                            act.wait_ge(lc_ready, which[0] + 1)
                            nc.scalar.activation(lc[:], lc[:], ACT.Exp).then_inc(lc_exp, 1)
                        chunk += what in ("tile", "out") and which[-1]

            def ffn(layer):
                base = START[f"ffn{layer}"]

                def gate_silu(f, parity):
                    act.wait_ge(gate_scaled, f + (layer * FT + 1))
                    nc.scalar.activation(silu[:, parity], silu[:, parity], ACT.Silu).then_inc(silu_ready, 1)

                def hidden_hi(f, parity):
                    act.wait_ge(hid_ready, f + (layer * FT + 1))
                    nc.scalar.copy(hid_hi[:, parity], hid[:, parity]).then_inc(hid_hi_ready, 1)

                gained(f"f{layer}")
                square(f"f{layer}")
                split_to(base + 1 + AHEAD)
                root(f"f{layer}")
                split_to(base + 2 + AHEAD)
                gate_silu(0, 0)
                hidden_hi(0, 0)
                split_to(base + 4 + AHEAD)
                gate_silu(1, 1)
                hidden_hi(1, 1)
                if layer == 0:
                    gained("mem1")
                split_to(base + 5 + AHEAD)
                with act.Fori(0, FFN_LOOPS) as i:
                    k = [0]
                    for j in (0, 1):
                        split_loop(i, k, 1)
                        gate_silu(i * 2 + (2 + j), j)
                        split_loop(i, k, 1)
                        hidden_hi(i * 2 + (2 + j), j)
                        split_loop(i, k, 1)
                split[0] += FFN_LOOPS * RING
                for f in (FT - 2, FT - 1):
                    split_to(base + 3 * f + 1 + AHEAD)
                    gate_silu(f, f % 2)
                    hidden_hi(f, f % 2)
                if layer == 0:
                    split_to(LAST_DOWN[0] + 1 + AHEAD)

            act.wait_ge(consts_set, 2)
            nc.scalar.activation(warm[:], eps[:], ACT.Sqrt)
            split_to(1)
            gained("mem0")
            split_to(2)
            square("mem0")
            split_to(3)
            gained("x0")
            split_to(4)
            root("mem0")
            split_to(6)
            square("x0")
            split_to(START["mem_v0"] + 3)
            columns(1, 0)
            split_to(START["conv"] + 3)
            root("x0")
            act.wait_ge(rcol_copied, 1)
            copy_rows("mem_v0", [mv[:, t] for t in range(TT)], (2, 3), 0)

            split_to(START["conv"] + AHEAD)
            with act.Fori(0, KT // 2) as i:
                k = [0]
                for j in (0, 1):
                    split_loop(i, k, 2)
                    act.wait_ge(chunk_done, i * RING + (START["conv"] + 3 * j + 2))
                    nc.scalar.copy(c_sb[:, j], bank[j][:, 0:S]).then_inc(c_copied, 1)
                    split_loop(i, k, 1)
                    act.wait_ge(tok_ready, i * 2 + (j + 1))
                    nc.scalar.copy(mix_hi[:, bass.ds(i * 2 + j, 1)], conv[:, j:j + 1]).then_inc(tok_hi, 1)
            split[0] += 3 * KT
            act.wait_ge(table_stored, 16)
            attention(0)
            split_to(START["ffn0"] + AHEAD)
            ffn(0)

            gained("x1")
            square("x1")
            split_to(START["cmp_k"] + AHEAD)
            root("x1")
            copy_rows("mem_v1", [mv[:, t] for t in range(TT)], (0, 1), 0)
            for kv, w1 in enumerate(("w1_k", "w1_v")):
                split_to(START[("cmp_k", "cmp_v")[kv]] + 2 + AHEAD)
                act.wait_ge(blocks_ready, kv + 1)
                nc.scalar.copy(r_split[:, :, 0], r_raw).then_inc(blocks_hi, 1)
                if kv == 0:
                    split_to(START["w1_k"] + AHEAD)
                    columns(2, 1)
                    nc.scalar.mul(rcol[:, 2], bank[7][:, 0:TT], -1.0).then_inc(rcol_copied, 1)
                split_to(START[w1] + 2 + AHEAD)
                act.wait_ge(hmid_summed, kv + 1)
                nc.scalar.activation(hmid[:, kv], hmid[:, kv], ACT.Silu).then_inc(hmid_ready, 1)
            split_to(START["gates"] + 1 + AHEAD)
            act.wait_ge(chunk_done, START["gates"] + 1)
            act.wait_ge(rcol_copied, 3)
            for t in range(TT):
                ins = nc.scalar.activation(gate[:, t].rearrange("p b h -> p (b h)"),
                                           bank[6][:, t * 3 * H:(t + 1) * 3 * H], ACT.Exp, scale=rcol[:, 2, t:t + 1])
            ins.then_inc(gate_exp, 1)
            copy_rows("nat_v", [v_nat[:, t].rearrange("p b g d -> p (b g d)") for t in range(TT)], (2, 3), 1)
            attention(1)
            split_to(START["ffn1"] + AHEAD)
            ffn(1)
            nc.scalar.activation(warm[:], eps[:], ACT.Sqrt)
            square("end")
            for m in range(KT):
                nc.scalar.mul(mem[:, m], h[:, m], gain[:, NORMS.index("end"), m:m + 1]).then_inc(out_gained, 1)
                if m == 3:
                    root("end")

        @block.vector
        def _(dve):
            split = [0]
            steps = [0]

            def link(ins):
                steps[0] += 1
                ins.then_inc(dve_step, 1)
                dve.wait_ge(dve_step, steps[0])

            def split_lo(c, slot):
                dve.wait_ge(hi_ready, c + 1)
                nc.vector.tensor_tensor(w_lo[:, slot], raw[:, slot % RAW], f32(w_hi[:, slot]), ALU.subtract)\
                    .then_inc(lo_ready, 1)

            def split_to(end):
                while split[0] < min(end, TOTAL):
                    split_lo(split[0], split[0] % RING)
                    split[0] += 1

            def split_loop(i, k, count):
                for _ in range(count):
                    c = split[0] + k[0]
                    split_lo(i * RING + c, c % RING)
                    k[0] += 1

            his = [0]
            residuals = [0]

            def add_residual(done, b):
                if b < 3:
                    dve.wait_ge(bank_done, residuals[0] // 4 * 3 + b + 1)
                else:
                    dve.wait_ge(chunk_done, done)
                hh = h[:, 2 * b:2 * b + 2]
                nc.vector.tensor_tensor(hh, bank[b][:].rearrange("p (m s) -> p m s", m=2), hh, ALU.add)\
                    .then_inc(residual_added, 1)
                residuals[0] += 1

            def gained_lo(name, m):
                src, hi, lo = (mem, m_hi, m_lo) if name.startswith("mem") else (h, n_hi, n_lo)
                dve.wait_ge(gain_loaded, 16)
                if name == "x0":
                    dve.wait_ge(x_loaded, 16)
                elif not name.startswith("mem"):
                    dve.wait_ge(residual_added, KT // 2 * (SUMMED.index(name) - 2) + m // 2 + 1)
                dve.wait_ge(n_hi_ready, his[0] + 1)
                nc.vector.scalar_tensor_tensor(out=lo[:, m], in0=src[:, m],
                                               scalar=gain[:, NORMS.index(name), m:m + 1], in1=f32(hi[:, m]),
                                               op0=ALU.mult, op1=ALU.subtract).then_inc(n_lo_ready, 1)
                his[0] += 1

            def add_squares(name):
                k = SUMMED.index(name)
                dve.wait_ge(sq_ready, KT // 2 * k + 2)
                if k:
                    dve.wait_ge(sum_ready, k)
                nc.vector.tensor_tensor(sq_sum[:], sq[name][0][:], sq[name][1][:], ALU.add).then_inc(sq_added, 1)
                for m in (2, 3):
                    dve.wait_ge(sq_ready, KT // 2 * k + m + 1)
                    dve.wait_ge(sq_added, ADDS * k + m - 1)
                    nc.vector.tensor_tensor(sq_sum[:], sq_sum[:], sq[name][m][:], ALU.add).then_inc(sq_added, 1)
                dve.wait_ge(sq_added, ADDS * k + 3)
                nc.vector.tensor_tensor(sq_sum[:, 0], sq_sum[:, 0], sq_sum[:, 1], ALU.add).then_inc(sq_added, 1)

            def inverse(name):
                k = SUMMED.index(name)
                dve.wait_ge(rms_ready, k + 1)
                nc.vector.reciprocal((mem_rstd if name == "mem0" else rstd)[:], rms[:]).then_inc(rstd_ready, 1)
                dve.wait_ge(rstd_ready, k + 1)

            def residual_and_gain(done, name):
                add_residual(done, 0)
                for b in range(4):
                    if b < 3:
                        add_residual(done, b + 1)
                    for m in (2 * b, 2 * b + 1):
                        if name != "end":
                            gained_lo(name, m)
                add_squares(name)

            tiles = [0]

            def copy_tile(c, out, scale, banks=(0, 1)):
                dve.wait_ge(chunk_done, c + 1)
                tile = bank[banks[tiles[0] % len(banks)]][:, 0:S]
                nc.vector.scalar_tensor_tensor(out=out, in0=tile, scalar=scale, in1=rstd[:],
                                               op0=ALU.mult, op1=ALU.mult).then_inc(tile_copied, 1)
                tiles[0] += 1

            def copy_tiles(part, first, end, banks=(0, 1)):
                for n in range(first, end):
                    split_to(START[part] + n + AHEAD)
                    copy_tile(START[part] + n, *tile_target(part, n), banks)

            def memory_keys(layer, pair):
                dve.wait_ge(chunk_done, KEY_CHUNKS[layer][2 * pair + 1] + 1)
                keys = bank[4 + pair][:].rearrange("p (a m) -> p a m", a=2)
                nc.vector.tensor_tensor(mk[:, 2 * pair:2 * pair + 2], keys,
                                        mem_rstd[:, None].to_broadcast([P, 2, M]), ALU.mult).then_inc(mk_copied, 1)

            def largest(n):
                u, k, b = UNITS[n], n % 3, bank[4 + n % 2]
                dve.wait_ge(scores_ready, n + 1)
                if u[0] == "mem":
                    if n >= 3:
                        dve.wait_ge(turned, n - 2)
                    nc.vector.reduce_max(col[:, k, 0, 0:1], b[:, 0:M], AX_X, negate=True).then_inc(max_ready, 1)
                    return
                keys, head = (u[2] + 1) * P, u[1] * HPG + u[3]
                dve.wait_ge(turned, n - 2)
                link(nc.vector.tensor_tensor(att[:, k, :, 0:keys], b[:].rearrange("p (b s) -> p b s", b=2)[:, :, 0:keys],
                                             bias[:, head, None, keys - 1::-1].to_broadcast([P, 2, keys]), ALU.add))
                nc.vector.reduce_max(col[:, k, 0], att[:, k, :, 0:keys], AX_X, negate=True).then_inc(max_ready, 1)

            def scale(n):
                u, k = UNITS[n], n % 3
                dve.wait_ge(exp_ready, n + 1)
                if u[0] == "mem":
                    link(nc.vector.reciprocal(col[:, k, 2, 0:1], col[:, k, 1, 0:1]))
                    nc.vector.tensor_scalar(att[:, k, 0], att[:, k, 0], col[:, k, 2, 0:1], None, ALU.mult)\
                        .then_inc(prob_ready, 1)
                    return
                keys, head = (u[2] + 1) * P, u[1] * HPG + u[3]
                link(nc.vector.reciprocal(col[:, k, 2], col[:, k, 1]))
                link(nc.vector.tensor_tensor(col[:, k, 3], col[:, k, 2], gate[:, u[2], 1:3, head], ALU.mult))
                for br in range(2):
                    ins = nc.vector.tensor_scalar(att[:, k, br, 0:keys], att[:, k, br, 0:keys],
                                                  col[:, k, 3, br:br + 1], None, ALU.mult)
                ins.then_inc(prob_ready, 1)

            def output_lo(n):
                if not makes_output(n):
                    return
                dve.wait_ge(out_hi, outputs_before(n) + 1)
                nc.vector.tensor_tensor(output_of(n, mix_lo), output_psum(n), f32(output_of(n, mix_hi)),
                                        ALU.subtract).then_inc(out_lo, 1)

            def compressed(pair):
                dve.wait_ge(sc_ready, pair + 1)
                if pair:
                    dve.wait_ge(pc_ready, pair)
                    dve.wait_ge(pcT_ready, pair)
                heads = slice(2 * HPG * pair, 2 * HPG * (pair + 1))
                lcs = lc[:].rearrange("p (t o a) c -> p t o (a c)", t=TT, o=2)
                biases = bias_c[:, :, heads].rearrange("p t (o a) c -> p t o (a c)", o=2)
                for odd in range(2):
                    ins = nc.vector.tensor_tensor(lcs[:, :, odd], cmp_bank(odd)[:, 0:TT * HPG * NC].rearrange(
                        "p (t x) -> p t x", t=TT), biases[:, :, odd], ALU.add)
                link(ins)
                link(nc.vector.reduce_max(colc[:, 0], lc[:], AX_X))
                link(nc.vector.tensor_scalar(colc[:, 1], colc[:, 0], NEG / 10, None, ALU.max))
                nc.vector.tensor_tensor(lc[:], lc[:], colc[:, 1, :, None].to_broadcast([P, H, NC]), ALU.subtract)\
                    .then_inc(lc_ready, 1)
                dve.wait_ge(lc_exp, pair + 1)
                link(nc.vector.reduce_sum(colc[:, 2], lc[:], AX_X))
                link(nc.vector.tensor_scalar(colc[:, 2], colc[:, 2], 1e-30, None, ALU.max))
                link(nc.vector.reciprocal(colc[:, 3], colc[:, 2]))
                scaled = colc[:, 3].rearrange("p (t h) -> p t h", t=TT)
                link(nc.vector.tensor_tensor(scaled, scaled, gate[:, :, 0, heads], ALU.mult))
                nc.vector.tensor_tensor(pc[:, :, 0:NC], lc[:], colc[:, 3, :, None].to_broadcast([P, H, NC]), ALU.mult)\
                    .then_inc(pc_ready, 1)

            def attention(layer):
                chunk = START["out0"] if layer == 0 else START["kq1"]
                for n, beside in steps_of(layer):
                    if is_unit(layer, n - 5):
                        output_lo(n - 5)
                    if is_unit(layer, n):
                        largest(n)
                    split_to(chunk + AHEAD)
                    if is_unit(layer, n - 1):
                        scale(n - 1)
                    for what, *which in beside:
                        if what == "tile" and which[-1]:
                            copy_tile(chunk, *tile_target(*which[:-1]))
                        elif what == "cmp_scores":
                            compressed(*which)
                        elif what == "cmp_turn":
                            pair = which[0]
                            dve.wait_ge(pcT_ready, pair + 1)
                            nc.vector.tensor_copy(pcT[:, 4 * pair:4 * pair + 4],
                                                  bank[2][:].rearrange("p (u q) -> p u q", q=P)).then_inc(pcT_copied, 1)
                        chunk += what in ("tile", "out") and which[-1]

            def ffn(layer):
                base = START[f"ffn{layer}"]

                def scale_gate_up(f, parity, done):
                    dve.wait_ge(chunk_done, done)
                    if not (layer == 0 and isinstance(f, int) and f < 2):
                        dve.wait_ge(hid_lo_ready, f + (layer * FT - 1))
                    nc.vector.tensor_tensor(silu[:, parity], bank[4 + parity][:, 0:S], rstd[:], ALU.mult)\
                        .then_inc(gate_scaled, 1)
                    nc.vector.tensor_tensor(hid[:, parity], bank[4 + parity][:, S:2 * S], rstd[:], ALU.mult)\
                        .then_inc(up_scaled, 1)

                def hidden(f, parity):
                    count = f + (layer * FT + 1)
                    dve.wait_ge(up_scaled, count)
                    dve.wait_ge(silu_ready, count)
                    nc.vector.tensor_tensor(hid[:, parity], hid[:, parity], silu[:, parity], ALU.mult)\
                        .then_inc(hid_ready, 1)

                def hidden_lo(f, parity):
                    dve.wait_ge(hid_hi_ready, f + (layer * FT + 1))
                    nc.vector.tensor_tensor(hid_lo[:, parity], hid[:, parity], f32(hid_hi[:, parity]), ALU.subtract)\
                        .then_inc(hid_lo_ready, 1)

                name = f"f{layer}"
                residual_and_gain(START[f"out{layer}"] + MIXT, name)
                split_to(base + 1 + AHEAD)
                inverse(name)
                for f in (0, 1):
                    scale_gate_up(f, f, base + 2 + 2 * f)
                    split_to(base + 2 + 2 * f + AHEAD)
                    hidden(f, f)
                    hidden_lo(f, f)
                if layer == 0:
                    for m in range(KT):
                        gained_lo("mem1", m)
                split_to(base + 5 + AHEAD)
                with dve.Fori(0, FFN_LOOPS) as i:
                    k = [0]
                    for j in (0, 1):
                        f = i * 2 + (2 + j)
                        split_loop(i, k, 1)
                        scale_gate_up(f, j, i * RING + (base + 5 + 3 * j + 2))
                        split_loop(i, k, 1)
                        hidden(f, j)
                        split_loop(i, k, 1)
                        hidden_lo(f, j)
                split[0] += FFN_LOOPS * RING
                for f in (FT - 2, FT - 1):
                    scale_gate_up(f, f % 2, base + 3 * f + 1)
                    split_to(base + 3 * f + 1 + AHEAD)
                    hidden(f, f % 2)
                    hidden_lo(f, f % 2)
                if layer == 0:
                    split_to(LAST_DOWN[0] + 1 + AHEAD)
                residual_and_gain(LAST_DOWN[layer] + 1, "x1" if layer == 0 else "end")

            split_to(1)
            for m in range(KT):
                gained_lo("mem0", m)
            split_to(2)
            add_squares("mem0")
            split_to(3)
            for m in range(KT):
                gained_lo("x0", m)
            split_to(4)
            inverse("mem0")
            split_to(6)
            add_squares("x0")
            split_to(START["mem_v0"] + 3)
            memory_keys(0, 0)
            memory_keys(0, 1)
            split_to(START["conv"] + 3)
            inverse("x0")
            link(nc.vector.tensor_tensor(rstd_sq[:], rstd[:], rstd[:], ALU.mult))
            dve.wait_ge(table_ready, 1)
            nc.vector.tensor_copy(tab_row, bank[6][0:H, :]).then_inc(table_copied, 1)
            split_to(START["conv"] + AHEAD)
            per = 2 * 6
            conv_steps = steps[0]
            with dve.Fori(0, KT // 2) as i:
                k = [0]
                done = [0]

                def chain(ins):
                    done[0] += 1
                    ins.then_inc(dve_step, 1)
                    dve.wait_ge(dve_step, i * per + (conv_steps + done[0]))

                for j in (0, 1):
                    ft = i * 2 + j
                    split_loop(i, k, 2)
                    dve.wait_ge(c_copied, ft + 1)
                    chain(nc.vector.tensor_tensor(vpad[:, j, 2:S + 2], bank[j][:, S:2 * S], c_sb[:, j], ALU.mult))
                    chain(nc.vector.tensor_tensor(vpad[:, j, 2:S + 2], vpad[:, j, 2:S + 2], rstd_sq[:], ALU.mult))
                    chain(nc.vector.tensor_scalar(conv[:, j], vpad[:, j, 0:S], taps[:, 0, bass.ds(ft, 1)], None, ALU.mult))
                    for tap in (1, 2):
                        chain(nc.vector.scalar_tensor_tensor(out=conv[:, j], in0=vpad[:, j, tap:tap + S],
                                                             scalar=taps[:, tap, bass.ds(ft, 1)], in1=conv[:, j],
                                                             op0=ALU.mult, op1=ALU.add))
                    chain(nc.vector.tensor_tensor(conv[:, j], conv[:, j], rstd[:], ALU.mult))
                    dve.wait_ge(chunk_done, i * RING + (START["conv"] + 3 * j + 3))
                    nc.vector.tensor_tensor(conv[:, j], bank[4 + j][:, 0:S], conv[:, j], ALU.mult).then_inc(tok_ready, 1)
                    split_loop(i, k, 1)
                    dve.wait_ge(tok_hi, ft + 1)
                    nc.vector.tensor_tensor(mix_lo[:, bass.ds(ft, 1)], conv[:, j:j + 1], f32(mix_hi[:, bass.ds(ft, 1)]),
                                            ALU.subtract).then_inc(tok_lo, 1)
                    dve.wait_ge(tok_lo, ft + 1)
                assert done[0] == per
            steps[0] += per * (KT // 2)
            split[0] += 3 * KT
            copy_tiles("xq0", 0, XH, (2, 3, 6, 7))
            attention(0)
            split_to(START["ffn0"] + AHEAD)
            ffn(0)

            split_to(KEY_CHUNKS[1][2] + 1 + AHEAD)
            memory_keys(1, 0)
            memory_keys(1, 1)
            split_to(START["cmp_k"] + AHEAD)
            inverse("x1")
            split_to(START["cmp_k"] + AHEAD)

            def blocks(kv, part):
                for pair in range(2):
                    dve.wait_ge(chunk_done, START[part] + pair + 1)
                    link(nc.vector.tensor_tensor(silu[:, pair], bank[2 + pair][:, 0:S], rstd[:], ALU.mult))
                    for gg in range(2):
                        for half in range(2):
                            src = silu[64 * gg:64 * gg + 64, pair, CS * half:CS * (half + NC)]
                            at = slice(64 * half, 64 * half + 64)
                            ins = nc.vector.tensor_tensor(
                                r_raw[at, :, (2 * pair + gg) * NC:(2 * pair + gg + 1) * NC],
                                src.rearrange("p (c l) -> p l c", l=CS),
                                pos[at, kv, :, None].to_broadcast([64, CS, NC]), ALU.add)
                ins.then_inc(blocks_ready, 1)

            def blocks_low(kv):
                dve.wait_ge(blocks_hi, kv + 1)
                nc.vector.tensor_tensor(r_split[:, :, 1], r_raw, f32(r_split[:, :, 0]), ALU.subtract).then_inc(blocks_lo, 1)

            def hidden_sum(kv, part):
                parts = bank[4][:, 0:2 * G * NC].rearrange("p (b x) -> p b x", b=2)
                dve.wait_ge(chunk_done, START[part] + 2)
                nc.vector.tensor_copy(hmid[:, kv], parts[:, 0]).then_inc(hmid_copied, 1)
                dve.wait_ge(hmid_copied, kv + 1)
                nc.vector.tensor_tensor(hmid[:, kv], hmid[:, kv], parts[:, 1], ALU.add).then_inc(hmid_summed, 1)

            split_to(START["cmp_k"] + 2 + AHEAD)
            blocks(0, "cmp_k")
            copy_tiles("kq0", 0, 1, (0, 1, 6))
            blocks_low(0)
            copy_tiles("kq0", 1, 3, (0, 1, 6))
            split_to(START["cmp_v"] + AHEAD)
            hidden_sum(0, "w1_k")
            split_to(START["cmp_v"] + 2 + AHEAD)
            dve.wait_ge(blocks_lo, 1)
            blocks(1, "cmp_v")
            dve.wait_ge(kvc_ready, 1)
            nc.vector.tensor_copy(kc[:], bank[5][:, 0:G * NC].rearrange("p (g c) -> p g c", g=G))\
                .then_inc(kvc_copied, 1)
            copy_tiles("q0", 0, 1, (0, 1, 6))
            dve.wait_ge(chunk_done, START["w1_k"] + 2)
            blocks_low(1)
            copy_tiles("q0", 1, 3, (0, 1, 6))
            split_to(START["gates"] + AHEAD)
            hidden_sum(1, "w1_v")
            dve.wait_ge(consts_set, CONSTS)
            dve.wait_ge(kvc_ready, 2)
            for a in range(HPG):
                nc.vector.tensor_copy(vc[32 * a:32 * a + NC, :, a * DK:(a + 1) * DK],
                                      bank[5][0:NC, 0:G * DK].rearrange("p (g d) -> p g d", g=G))\
                    .then_inc(kvc_copied, 1)
            split_to(START["gates"] + 1 + AHEAD)
            dve.wait_ge(gate_exp, 1)
            link(nc.vector.tensor_scalar(gate[:], gate[:], 1.0, None, ALU.add))
            link(nc.vector.reciprocal(gate[:], gate[:]))
            split_to(START["nat_v"] + COUNT["nat_v"] + AHEAD)
            dve.wait_ge(bias_loaded, 16)
            dve.wait_ge(consts_set, CONSTS)
            for t in range(TT):
                last = (t + 1) * P - CB
                blocks_seen = min(NC, last // CS + 1)
                stop = last - blocks_seen * CS
                ins = nc.vector.tensor_copy(bias_c[:, t, :, 0:blocks_seen],
                                            bias[:, :, last:(None if stop < 0 else stop):-CS])
            link(ins)
            attention(1)
            split_to(START["ffn1"] + AHEAD)
            ffn(1)
            inverse("end")
            for n in range(DVE_PAIRS):
                dve.wait_ge(out_gained, 2 * n + 2)
                out = mem[:, 2 * n:2 * n + 2]
                nc.vector.tensor_tensor(out, out, rstd[:, None].to_broadcast([P, 2, S]), ALU.mult).then_inc(out_ready, 1)

        @block.tensor
        def _(pe):
            def half_of(half):
                return range(KT) if half is None else range(half * KT // 2, (half + 1) * KT // 2)

            def three_passes(out, slot, cols, x_hi, x_lo, start, stop, **kw):
                nc.tensor.matmul(out, w_hi[:, slot, cols], x_hi, start=start, stop=False, **kw)
                nc.tensor.matmul(out, w_hi[:, slot, cols], x_lo, start=False, stop=False, **kw)
                return nc.tensor.matmul(out, w_lo[:, slot, cols], x_hi, start=False, stop=stop, **kw)

            def project(c, slot, out, x_hi, x_lo, normed=None, half=None):
                pe.wait_ge(lo_ready, c + 1)
                for kt in half_of(half):
                    if normed is not None:
                        pe.wait_ge(n_lo_ready, normed * KT + kt + 1)
                    ins = three_passes(out, slot, slice(kt * P, kt * P + P), x_hi[:, kt], x_lo[:, kt],
                                       kt == 0, kt == KT - 1)
                if half != 0:
                    ins.then_inc(chunk_done, 1)

            copied = [0]

            def project_tile(c, x_hi, x_lo, banks=(0, 1), half=None):
                if copied[0] >= len(banks):
                    pe.wait_ge(tile_copied, copied[0] - len(banks) + 1)
                project(c, c % RING, bank[banks[copied[0] % len(banks)]][:, 0:S], x_hi, x_lo, None, half)
                copied[0] += half != 0

            def project_tiles(part, x_hi, x_lo, banks=(0, 1)):
                for n in range(COUNT[part]):
                    project_tile(START[part] + n, x_hi, x_lo, banks)

            def project_rows(part, x_hi, x_lo, banks):
                for j in range(4):
                    c = START[part] + j
                    slot = c % RING
                    pe.wait_ge(lo_ready, c + 1)
                    for kt in (2 * j, 2 * j + 1):
                        cols = slice(kt % 2 * 512, kt % 2 * 512 + 512)
                        for t in range(TT):
                            at = slice(t * P, t * P + P)
                            out = bank[banks[t]][:]
                            nc.tensor.matmul(out, x_hi[:, kt, at], w_hi[:, slot, cols], start=kt == 0, stop=False)
                            nc.tensor.matmul(out, x_lo[:, kt, at], w_hi[:, slot, cols], start=False, stop=False)
                            ins = nc.tensor.matmul(out, x_hi[:, kt, at], w_lo[:, slot, cols],
                                                   start=False, stop=kt == KT - 1)
                    ins.then_inc(chunk_done, 1)

            squares = [0]

            def sum_squares():
                k = squares[0]
                pe.wait_ge(sq_added, ADDS * (k + 1))
                if k:
                    pe.wait_ge(rms_ready, k)
                if k >= 2:
                    pe.wait_ge(out_lo, outputs_before(FIRST_UNIT[k // 2]))
                nc.tensor.matmul(bank[7][:, 0:S], ones[:], sq_sum[:, 0], start=True, stop=True).then_inc(sum_ready, 1)
                squares[0] += 1

            def accumulate(c, slot, x_hi, x_lo, first, last, half=None):
                pe.wait_ge(lo_ready, c + 1)
                for m in half_of(half):
                    ins = three_passes(bank[m // 2][:, m % 2 * S:m % 2 * S + S], slot, slice(m * P, m * P + P),
                                       x_hi, x_lo, first and m % 2 == 0, last, skip_group_check=True)
                    if last and m % 2 and m < KT - 1:
                        ins.then_inc(bank_done, 1)
                if half != 0:
                    ins.then_inc(chunk_done, 1)

            def query(g, a, t):
                return q_sb[64 * (g % 2):64 * (g % 2) + 64, 4 * (g // 2) + a, t * P:t * P + P]

            def scores(n):
                u, b = UNITS[n], bank[4 + n % 2]
                if n >= 2:
                    pe.wait_ge(exp_ready if UNITS[n - 2][0] == "mem" else max_ready, n - 1)
                if n < FIRST_UNIT[1]:
                    pe.wait_ge(tile_copied, u[1] + 1)
                if u[0] == "mem":
                    nc.tensor.matmul(b[:, 0:M], xq[:, u[1], u[2] * P:u[2] * P + P], mk[:, u[1]],
                                     start=True, stop=True).then_inc(scores_ready, 1)
                    return
                g, t, a = u[1:]
                for br in range(2):
                    ins = nc.tensor.matmul(b[:, br * S:br * S + (t + 1) * P], query(g, a, t),
                                           ks[64 * (g % 2):64 * (g % 2) + 64, br, g // 2, 0:(t + 1) * P],
                                           start=True, stop=True)
                ins.then_inc(scores_ready, 1)

            def turn(n):
                pe.wait_ge(prob_ready, n + 1)
                if n:
                    pe.wait_ge(probT_ready, n)
                blocks = keys_of(n)
                for at in range(blocks):
                    br, kt = (0, at) if UNITS[n][0] == "mem" else divmod(at, blocks // 2)
                    ins = nc.tensor.transpose(bank[6][:, at * P:at * P + P],
                                              att[:, n % 3, br, kt * P:kt * P + P], idt[:])
                ins.then_inc(turned, 1)

            def values(n):
                u = UNITS[n]
                if u[0] == "mem" and not makes_output(n):
                    return
                pe.wait_ge(probT_ready, n + 1)
                if outputs_before(n) and (u[0] == "mem" or u[3] == 0):
                    pe.wait_ge(out_lo, outputs_before(n))
                if u[0] == "mem":
                    for m in range(2):
                        ins = nc.tensor.matmul(bank[7][:, 0:S], mv[:, m, u[1] * P:u[1] * P + P], xprobT[:, m],
                                               start=m == 0, stop=m == 1)
                    ins.then_inc(values_done, 1)
                    return
                g, t, a = u[1:]
                if a == 0:
                    pe.wait_ge(pcT_copied, g // 2 + 1)
                    for half in range(2):
                        nc.tensor.matmul(bank[7][:, half * P:half * P + P], vc[:, g, half * P:half * P + P],
                                         pcT[:, g * TT + t], start=half == 0, stop=False, skip_group_check=True)
                for br in range(2):
                    for kt in range(t + 1):
                        last = a == HPG - 1 and br == 1 and kt == t
                        ins = nc.tensor.matmul(bank[7][DK * (a % 2):DK * (a % 2) + DK, a // 2 * P:a // 2 * P + P],
                                               v_nat[:, kt, br, g], probT[:, n % 2, br * (t + 1) + kt],
                                               start=False, stop=last, skip_group_check=True)
                ins.then_inc(values_done, 1)

            def compressed_scores(pair):
                pe.wait_ge(kvc_copied, 1 + HPG)
                pe.wait_ge(rows_copied, 3 * TT)
                if pair:
                    pe.wait_ge(pcT_copied, pair)
                for odd in range(2):
                    for t in range(TT):
                        for a in range(HPG):
                            at, g = t * HPG + a, 2 * pair + odd
                            ins = nc.tensor.matmul(cmp_bank(odd)[:, at * NC:(at + 1) * NC], query(g, a, t),
                                                   kc[64 * odd:64 * odd + 64, g], start=True, stop=True)
                ins.then_inc(sc_ready, 1)

            def compressed_turn(pair):
                pe.wait_ge(pc_ready, pair + 1)
                for k in range(2 * TT):
                    odd, t = divmod(k, TT)
                    at = (t * 2 + odd) * HPG
                    ins = nc.tensor.transpose(bank[2][:, k * P:k * P + P],
                                              pc[:, at:at + HPG].rearrange("p h c -> p (h c)"), idt[:])
                ins.then_inc(pcT_ready, 1)

            def mix_out(layer, j, half=None):
                c, kt = START[f"out{layer}"] + j, OUT_ORDER[layer][j]
                if j == 0:
                    pe.wait_ge(tile_copied, copied[0] if layer else 2)
                    pe.wait_ge(rows_copied, (3 if layer else 1) * TT)
                    pe.wait_ge(pcT_copied, 2) if layer else pe.wait_ge(tok_lo, KT)
                if layer or kt >= KT:
                    unit = [n for n in range(FIRST_UNIT[layer], FIRST_UNIT[layer + 1]) if makes_output(n)
                            and (UNITS[n][:2] == ("mem", kt - KT) if kt >= KT
                                 else UNITS[n][0] == "nsa" and UNITS[n][1] == kt // 2)][-1]
                    pe.wait_ge(out_lo, outputs_before(unit) + 1)
                accumulate(c, c % RING, mix_hi[:, kt], mix_lo[:, kt], j == 0, j == MIXT - 1, half)

            def attention(layer):
                chunk, outs = (START["out0"] if layer == 0 else START["kq1"]), 0
                for n, beside in steps_of(layer):
                    if is_unit(layer, n - 3):
                        turn(n - 3)
                    if is_unit(layer, n):
                        scores(n)
                    if is_unit(layer, n - 4) and UNITS[n - 4][-1] > 0:
                        values(n - 4)
                    for what, *which in beside:
                        if what == "tile":
                            project_tile(chunk, n_hi, n_lo, half=which[-1])
                        elif what == "out":
                            mix_out(layer, *which)
                            outs += which[-1]
                        elif what == "cmp_scores":
                            compressed_scores(*which)
                        else:
                            compressed_turn(*which)
                        chunk += what in ("tile", "out") and which[-1]
                    if is_unit(layer, n - 4) and UNITS[n - 4][-1] == 0:
                        values(n - 4)
                for j in range(outs, MIXT):
                    mix_out(layer, j)

            def ffn(layer):
                base = START[f"ffn{layer}"]

                def gate_up(f, parity, c, slot, normed=None):
                    if not (layer == 0 and isinstance(f, int) and f < 2):
                        pe.wait_ge(up_scaled, f + (layer * FT - 1))
                    for j in range(2):
                        project(c + j, (slot + j) % RING, bank[4 + parity][:, j * S:j * S + S], n_hi, n_lo,
                                normed if j == 0 else None)

                def down(f, parity, c, slot, first=False, last=False):
                    pe.wait_ge(hid_lo_ready, f + (layer * FT + 1))
                    accumulate(c, slot % RING, hid_hi[:, parity], hid_lo[:, parity], first, last)

                gate_up(0, 0, base, base, NORMS.index(f"f{layer}"))
                sum_squares()
                gate_up(1, 1, base + 2, base + 2)
                down(0, 0, base + 4, base + 4, first=True)
                with pe.Fori(0, FFN_LOOPS) as i:
                    for j in (0, 1):
                        c = base + 5 + 3 * j
                        gate_up(i * 2 + (2 + j), j, i * RING + c, c)
                        down(i * 2 + (1 + j), 1 - j, i * RING + (c + 2), c + 2)
                for f in (FT - 2, FT - 1):
                    c = base + 3 * f - 1
                    gate_up(f, f % 2, c, c)
                    down(f - 1, (f - 1) % 2, c + 2, c + 2)
                if layer == 0:
                    pe.wait_ge(up_scaled, FT - 1)
                    memory_key(1, 0)
                    memory_key(1, 1)
                down(FT - 1, (FT - 1) % 2, LAST_DOWN[layer], LAST_DOWN[layer], last=True)
                if layer == 0:
                    pe.wait_ge(up_scaled, FT)

            def memory_key(layer, a, normed=None):
                c = KEY_CHUNKS[layer][a]
                project(c, c % RING, bank[4 + a // 2][:, a % 2 * M:a % 2 * M + M], m_hi, m_lo, normed)

            def columns(norm, source):
                pe.wait_ge(rstd_ready, SUMMED.index(norm) + 1)
                pe.wait_ge(rms_ready, SUMMED.index(norm) + 1)
                for t in range(TT):
                    ins = nc.tensor.matmul(bank[7][:, t:t + 1], source[:, t * P:t * P + P], idt[:, 0:1],
                                           start=True, stop=True)
                ins.then_inc(rcol_ready, 1)

            memory_key(0, 0, NORMS.index("mem0"))
            memory_key(0, 1)
            pe.wait_ge(consts_set, CONSTS)
            sum_squares()
            memory_key(0, 2)
            memory_key(0, 3)
            pe.wait_ge(small_loaded, SMALL)
            nc.tensor.matmul(bank[6][0:H, :], tab[:], fwd, start=True, stop=True).then_inc(table_ready, 1)
            columns("mem0", mem_rstd)
            project_rows("mem_v0", m_hi, m_lo, (2, 3))
            pe.wait_ge(rcol_copied, 1)
            sum_squares()

            def conv_tile(j, c, slot, normed=None):
                project(c, slot % RING, bank[j][:, 0:S], n_hi, n_lo, normed)
                project(c + 1, (slot + 1) % RING, bank[j][:, S:2 * S], n_hi, n_lo)
                project(c + 2, (slot + 2) % RING, bank[4 + j][:, 0:S], n_hi, n_lo)

            pe.wait_ge(mk_copied, 2)
            base = START["conv"]
            for j in (0, 1):
                conv_tile(j, base + 3 * j, base + 3 * j, None if j else NORMS.index("x0"))
            with pe.Fori(1, KT // 2) as i:
                for j in (0, 1):
                    pe.wait_ge(tok_ready, i * 2 + (j - 1))
                    conv_tile(j, i * RING + (base + 3 * j), base + 3 * j)
            pe.wait_ge(rows_copied, TT)
            pe.wait_ge(table_copied, 1)
            pe.wait_ge(rms_ready, 2)
            project_tiles("xq0", n_hi, n_lo, (2, 3, 6, 7))
            pe.wait_ge(tok_ready, KT)
            attention(0)
            ffn(0)

            memory_key(1, 2)
            memory_key(1, 3)
            pe.wait_ge(residual_added, KT - 2)
            project_rows("mem_v1", m_hi, m_lo, (0, 1))
            pe.wait_ge(residual_added, KT)
            sum_squares()

            def raw_blocks(part, normed=None):
                for pair in range(2):
                    c = START[part] + pair
                    project(c, c % RING, bank[2 + pair][:, 0:S], n_hi, n_lo, None if pair else normed)

            def hidden(kv, part):
                pe.wait_ge(blocks_lo, kv + 1)
                for j in range(2):
                    c = START[part] + j
                    pe.wait_ge(lo_ready, c + 1)
                    for l in range(8):
                        ll = 8 * j + l
                        cols = slice(l * P, l * P + P)
                        nc.tensor.matmul(bank[4][:, 0:2 * G * NC], w_hi[:, c % RING, cols],
                                         r_split[:, ll].rearrange("p b x -> p (b x)"), start=ll == 0, stop=False,
                                         skip_group_check=True)
                        ins = nc.tensor.matmul(bank[4][:, 0:G * NC], w_lo[:, c % RING, cols], r_split[:, ll, 0],
                                               start=False, stop=ll == CS - 1, skip_group_check=True)
                    ins.then_inc(chunk_done, 1)

            raw_blocks("cmp_k", NORMS.index("x1"))
            pe.wait_ge(rows_copied, 2 * TT)
            project_tiles("kq0", n_hi, n_lo, (0, 1, 6))
            columns("x1", rstd)
            pe.wait_ge(mk_copied, 4)
            hidden(0, "w1_k")
            pe.wait_ge(blocks_ready, 1)
            raw_blocks("cmp_v")
            pe.wait_ge(hmid_ready, 1)
            nc.tensor.matmul(bank[5][:, 0:G * NC], w2[:, 0], hmid[:, 0], start=True, stop=True).then_inc(kvc_ready, 1)
            project_tiles("q0", n_hi, n_lo, (0, 1, 6))
            hidden(1, "w1_v")
            c = START["gates"]
            pe.wait_ge(lo_ready, c + 1)
            pe.wait_ge(tile_copied, copied[0])
            for t in range(TT):
                at, out = slice(t * P, t * P + P), bank[6][:, t * 3 * H:(t + 1) * 3 * H]
                for kt in range(KT):
                    cols = slice(kt * 3 * H, (kt + 1) * 3 * H)
                    nc.tensor.matmul(out, n_hi[:, kt, at], w_hi[:, c % RING, cols], start=kt == 0, stop=False)
                    nc.tensor.matmul(out, n_lo[:, kt, at], w_hi[:, c % RING, cols], start=False, stop=False)
                    ins = nc.tensor.matmul(out, n_hi[:, kt, at], w_lo[:, c % RING, cols], start=False, stop=kt == KT - 1)
            ins.then_inc(chunk_done, 1)
            pe.wait_ge(hmid_ready, 2)
            pe.wait_ge(kvc_copied, 1)
            for g in range(G):
                ins = nc.tensor.matmul(bank[5][0:NC, g * DK:(g + 1) * DK], hmid[:, 1, g * NC:(g + 1) * NC],
                                       w2[:, 1, 0:DK], start=True, stop=True)
            ins.then_inc(kvc_ready, 1)
            pe.wait_ge(blocks_ready, 2)
            project_rows("nat_v", n_hi, n_lo, (2, 3))
            pe.wait_ge(rcol_copied, 3)
            pe.wait_ge(gate_exp, 1)
            attention(1)
            ffn(1)
            sum_squares()


def layout(x):
    def tiles(w):
        k, n = w.shape
        return w.reshape(k // P, P, n // P, P).transpose(2, 1, 0, 3).reshape(n // P, P, k)

    def rows(w):
        return w.reshape(4, 2, P, 512).transpose(0, 2, 1, 3).reshape(4, P, CHUNK)

    def by_input(w):
        return w.reshape(-1, P, CHUNK)

    conv, nsa = x["w_in_conv"][0], x["w_in_nsa"][0]
    kv0 = H * DK
    kvs = [nsa[:, kv0 + i * G * DK:kv0 + (i + 1) * G * DK] for i in range(6)]
    gates = nsa[:, kv0 + 6 * G * DK:kv0 + 6 * G * DK + 3 * H]
    q = nsa[:, :H * DK].reshape(D, G // 2, 2, HPG, DK).transpose(0, 1, 3, 2, 4).reshape(D, H * DK)
    gate_chunk = np.zeros((1, P, CHUNK), np.float32)
    gate_chunk[0, :, :KT * 3 * H] = gates.reshape(KT, P, 3 * H).transpose(1, 0, 2).reshape(P, KT * 3 * H)

    def w1(w):
        w = w.reshape(2, CS, DK, P).transpose(0, 2, 1, 3).reshape(P, 2, CHUNK)
        return w.transpose(1, 0, 2)

    def ffn(i):
        w = tiles(x["w_ffn_in"][i])
        gate, up, out = w[:FT], w[FT:], by_input(x["w_ffn_out"][i])
        parts = [gate[0], up[0]]
        for f in range(1, FT):
            parts += [gate[f], up[f], out[f - 1]]
        return np.stack(parts + [out[FT - 1]])

    b, c, u = (tiles(conv[:, i * D:(i + 1) * D]) for i in range(3))
    parts = {
        "conv": np.stack([c, u, b], 1).reshape(3 * KT, P, CHUNK),
        "xq0": tiles(conv[:, 3 * D:]), "xq1": tiles(nsa[:, -XH * P:]),
        "cmp_k": tiles(kvs[0]), "cmp_v": tiles(kvs[1]),
        "w1_k": w1(x["cmp_w1_k"][0]), "w1_v": w1(x["cmp_w1_v"][0]),
        "nat_v": rows(np.concatenate([kvs[3], kvs[5]], 1)), "gates": gate_chunk,
    }
    for i in range(2):
        parts[f"kq{i}"] = np.concatenate([tiles(kvs[2])[i:i + 1], tiles(kvs[4])[i:i + 1], tiles(q)[4 * i:4 * i + 4]])
        parts[f"mem_k{i}"] = tiles(x["w_mem_kv"][i][:, :XH * P])
        parts[f"mem_v{i}"] = rows(x["w_mem_kv"][i][:, XH * P:])
        parts[f"out{i}"] = by_input(x["w_out"][i])[OUT_ORDER[i]]
        parts[f"ffn{i}"] = ffn(i)
    parts["kq0"], parts["q0"] = parts["kq0"][:3], parts["kq0"][3:]
    parts["mem_k1"] = np.concatenate([parts["mem_k1"][:2], parts["ffn0"][-1:], parts["mem_k1"][2:]])
    parts["ffn0"] = parts["ffn0"][:-1]
    for name, count in PARTS:
        assert parts[name].shape == (count, P, CHUNK), name

    def features(a):
        return a.reshape(-1, KT, P).transpose(2, 1, 0)

    gains = np.stack([x["norm_mem_g"][0], x["norm_mix_g"][0], x["norm_ffn_g"][0],
                      x["norm_mem_g"][1], x["norm_mix_g"][1], x["norm_ffn_g"][1], x["norm_final_g"]])

    def positions(p):
        return p.reshape(2, CS, DK).transpose(0, 2, 1).reshape(P, CS)

    dist = np.arange(-DIST0, DIST0)
    near = BUCKETS // 2
    far = near + (np.log(np.maximum(dist, 1).astype(np.float32) / np.float32(near))
                  / np.float32(np.log(128 / near)) * (BUCKETS - near)).astype(np.int32)
    bucket = np.where(dist < 0, BUCKETS, np.where(dist < near, dist, np.minimum(far, BUCKETS - 1)))
    forward = (np.arange(BUCKETS + 1)[:, None] == bucket).astype(np.float32)
    return {
        "stream": np.concatenate([parts[name] for name, _ in PARTS]),
        "xT": features(x["x"][0]), "memT": features(x["mem"][0]),
        "gains": features(gains).transpose(0, 2, 1),
        "conv_w": features(x["conv_w"][0]).transpose(0, 2, 1),
        "cmp_pos": np.stack([positions(x["cmp_pos_k"][0]), positions(x["cmp_pos_v"][0])], 1),
        "cmp_w2": np.stack([np.concatenate([w[0], w[0]], 1) for w in (x["cmp_w2_k"], x["cmp_w2_v"])], 1),
        "rel_bias": x["rel_bias"], "dist_fwd": forward,
        "ident": np.eye(P, dtype=np.float32),
    }


def kernel(**inputs):
    import concourse.bacc as bacc
    from concourse.bass_utils import run_bass_kernel_spmd

    arrays = layout({k: np.asarray(v) for k, v in inputs.items()})
    arrays = {k: np.ascontiguousarray(v) for k, v in arrays.items()}
    nc = bacc.Bacc("TRN2", target_bir_lowering=False, num_devices=1)
    args = {k: nc.dram_tensor(k, a.shape, mybir.dt.from_np(a.dtype), kind="ExternalInput").ap()
            for k, a in arrays.items()}
    outT = nc.dram_tensor("outT", (P, KT, S), F32, kind="ExternalOutput").ap()
    build(nc, outT=outT, **args)
    got = run_bass_kernel_spmd(nc, [arrays], core_ids=[0]).results[0]["outT"]
    return np.ascontiguousarray(np.asarray(got).transpose(2, 1, 0).reshape(1, S, D))
```
